# Optimizing a Trainium2 kernel written in Bass

```python
import math
import jax, jax.numpy as jnp
from jax import lax
import numpy as np

D_MODEL = 1024
BATCH = 1
SEQ = 128
DEPTH = 2
DEC_BATCH = 1
DEC_SEQ = 256
PAST_LEN = 128

GRID_W = 64
HEAD_DIM = 64
NA_HEADS = 6
NA_WIN_ROWS = 8
NA_WIN_COLS = 16
RET_HEADS = 6
RET_CHUNK = 128
DIFF_HEADS = 4
DIFF_D = 32
DIFF_DV = 64
NA_W = NA_HEADS * HEAD_DIM
RET_W = RET_HEADS * HEAD_DIM
DIFF_W = DIFF_HEADS * DIFF_DV
MIX_W = NA_W + RET_W + DIFF_W
IN_SPLITS = (NA_W, NA_W, NA_W, RET_W, RET_W, RET_W, RET_W, DIFF_W, DIFF_W, DIFF_W)
IN_COLS = sum(IN_SPLITS)
N_GROUPS = 4
EXPERTS_PER_GROUP = 8
N_EXPERTS = N_GROUPS * EXPERTS_PER_GROUP
TOP_K_IN_GROUP = 2
EXPERT_FF = 256
Q_BLOCK = 128
ROPE_BASE = 10000.0
LN_EPS = 1e-5
NEG_INF = -1e30
ALPHA = (2.0 * DEPTH) ** 0.25
BETA = (8.0 * DEPTH) ** -0.25

kernel_name = 'hybrid_na_retention_diffattn_hmoe_flow_step'

def layer_norm(x, w, b):
    xf = x.astype(jnp.float32)
    mu = jnp.mean(xf, axis=-1, keepdims=True)
    var = jnp.mean(jnp.square(xf - mu), axis=-1, keepdims=True)
    return ((xf - mu) * lax.rsqrt(var + LN_EPS)).astype(x.dtype) * w + b

def head_layer_norm(o):
    of = o.astype(jnp.float32)
    mu = jnp.mean(of, axis=-1, keepdims=True)
    var = jnp.mean(jnp.square(of - mu), axis=-1, keepdims=True)
    return ((of - mu) * lax.rsqrt(var + LN_EPS)).astype(o.dtype)

def head_rms_norm(o):
    of = o.astype(jnp.float32)
    return (of * lax.rsqrt(jnp.mean(jnp.square(of), axis=-1, keepdims=True) + LN_EPS)).astype(o.dtype)

def modulation(cond, w_mod, b_mod):
    m = jax.nn.silu(cond) @ w_mod + b_mod
    return jnp.split(m[:, None, :], 6, axis=-1)

def axial_rope(x, pos_row, pos_col):
    half = x.shape[-1] // 2

    def rot(xa, pos):
        n = xa.shape[-1] // 2
        freqs = ROPE_BASE ** (-jnp.arange(n, dtype=jnp.float32) / n)
        ang = pos.astype(jnp.float32)[:, None] * freqs[None, :]
        ang = ang.reshape((ang.shape[0],) + (1,) * (xa.ndim - 3) + (n,))
        cos = jnp.cos(ang).astype(xa.dtype)
        sin = jnp.sin(ang).astype(xa.dtype)
        x1, x2 = xa[..., :n], xa[..., n:]
        return jnp.concatenate([x1 * cos - x2 * sin, x1 * sin + x2 * cos], axis=-1)

    return jnp.concatenate([rot(x[..., :half], pos_row), rot(x[..., half:], pos_col)], axis=-1)

def project(h, w_in):
    B, T, _ = h.shape
    p = h @ w_in
    bounds = np.cumsum((0,) + IN_SPLITS)
    parts = [p[..., int(bounds[i]):int(bounds[i + 1])] for i in range(len(IN_SPLITS))]
    na_q, na_k, na_v = [t.reshape(B, T, NA_HEADS, HEAD_DIM) for t in parts[0:3]]
    ret_q, ret_k, ret_v = [t.reshape(B, T, RET_HEADS, HEAD_DIM) for t in parts[3:6]]
    ret_k = ret_k * (HEAD_DIM ** -0.5)
    ret_g = parts[6]
    diff_q, diff_k = [t.reshape(B, T, DIFF_HEADS, 2, DIFF_D) for t in parts[7:9]]
    diff_v = parts[9].reshape(B, T, DIFF_HEADS, DIFF_DV)
    return na_q, na_k, na_v, ret_q, ret_k, ret_v, ret_g, diff_q, diff_k, diff_v

def _query_blocks(q):
    B, T = q.shape[:2]
    return jnp.moveaxis(q.reshape((B, T // Q_BLOCK, Q_BLOCK) + q.shape[2:]), 1, 0)

def _merge_blocks(o):
    nb, B = o.shape[:2]
    return jnp.moveaxis(o, 0, 1).reshape((B, nb * Q_BLOCK) + o.shape[3:])

def dense_attn(q, k, v):
    scale = q.shape[-1] ** -0.5

    def block(qb):
        s = jnp.einsum('bqhd,bkhd->bhqk', qb, k).astype(jnp.float32) * scale
        p = jax.nn.softmax(s, axis=-1).astype(v.dtype)
        return jnp.einsum('bhqk,bkhd->bqhd', p, v)

    return _merge_blocks(lax.map(block, _query_blocks(q)))

def diff_attn(q, k, v, lam):
    scale = q.shape[-1] ** -0.5

    def block(qb):
        s = jnp.einsum('bqhid,bkhid->bihqk', qb, k).astype(jnp.float32) * scale
        p = jax.nn.softmax(s, axis=-1)
        a = (p[:, 0] - lam * p[:, 1]).astype(v.dtype)
        return jnp.einsum('bhqk,bkhv->bqhv', a, v)

    return _merge_blocks(lax.map(block, _query_blocks(q)))

def diff_lambda_value(lam_p, lam_init):
    lp = lam_p.astype(jnp.float32)
    return jnp.exp(jnp.sum(lp[0] * lp[1])) - jnp.exp(jnp.sum(lp[2] * lp[3])) + lam_init

def retention_dir(q, k, v, log_g, s0, strict):
    B, T, H, dk = q.shape
    dv = v.shape[-1]
    n = T // RET_CHUNK
    idx = jnp.arange(RET_CHUNK, dtype=jnp.float32)
    dist = idx[:, None] - idx[None, :]
    mask = (dist > 0) if strict else (dist >= 0)
    intra = jnp.where(mask[None], jnp.exp(jnp.where(mask, dist, 0.0)[None] * log_g[:, None, None]), 0.0).astype(q.dtype)
    q_dec = jnp.exp((idx[:, None] + 1.0) * log_g[None, :]).astype(q.dtype)
    k_dec = jnp.exp((RET_CHUNK - 1.0 - idx[:, None]) * log_g[None, :]).astype(q.dtype)
    c_dec = jnp.exp(RET_CHUNK * log_g).astype(q.dtype)

    def step(S, inp):
        qb, kb, vb = inp
        sc = jnp.einsum('bihd,bjhd->bhij', qb, kb) * intra[None]
        inner = jnp.einsum('bhij,bjhv->bihv', sc, vb)
        cross = jnp.einsum('bihd,bhdv->bihv', qb, S) * q_dec[None, :, :, None]
        S_new = S * c_dec[None, :, None, None] + jnp.einsum('bjhd,bjhv->bhdv', kb * k_dec[None, :, :, None], vb)
        return S_new, inner + cross

    def split(t):
        return jnp.moveaxis(t.reshape((B, n, RET_CHUNK) + t.shape[2:]), 1, 0)

    S_fin, out = lax.scan(step, s0, (split(q), split(k), split(v)))
    return jnp.moveaxis(out, 0, 1).reshape(B, T, H, dv), S_fin

def retention_bidir(q, k, v, decay_logit, s0_fwd, s0_bwd):
    log_g = jax.nn.log_sigmoid(decay_logit.astype(jnp.float32))
    o_f, s_f = retention_dir(q, k, v, log_g[0], s0_fwd, False)
    flip = lambda t: jnp.flip(t, axis=1)
    o_b, s_b = retention_dir(flip(q), flip(k), flip(v), log_g[1], s0_bwd, True)
    return o_f + flip(o_b), s_f, s_b

def na_latent(q, k, v, k_ctx, v_ctx, rel_bias):
    B, T, H, d = q.shape
    rows = T // GRID_W
    wr = min(NA_WIN_ROWS, rows)
    scale = d ** -0.5
    r = jnp.arange(rows)
    row_start = jnp.clip(r - wr // 2, 0, rows - wr)
    row_idx = row_start[:, None] + jnp.arange(wr)[None, :]
    cidx = jnp.arange(GRID_W)
    col_start = jnp.clip(cidx - NA_WIN_COLS // 2, 0, GRID_W - NA_WIN_COLS)
    col_ok = (cidx[None, :] >= col_start[:, None]) & (cidx[None, :] < col_start[:, None] + NA_WIN_COLS)
    qg = q.reshape(B, rows, GRID_W, H, d)
    kg = k.reshape(B, rows, GRID_W, H, d)[:, row_idx]
    vg = v.reshape(B, rows, GRID_W, H, d)[:, row_idx]
    s_win = jnp.einsum('brqhd,brwkhd->bhrqwk', qg, kg).astype(jnp.float32) * scale
    dr = row_idx - r[:, None] + (NA_WIN_ROWS - 1)
    dc = jnp.clip(cidx[None, :] - cidx[:, None] + (NA_WIN_COLS - 1), 0, 2 * NA_WIN_COLS - 2)
    bias = rel_bias[:, dr[:, None, :, None], dc[None, :, None, :]]
    s_win = jnp.where(col_ok[:, None, :], s_win + bias[None].astype(jnp.float32), NEG_INF)
    s_ctx = jnp.einsum('brqhd,bkhd->bhrqk', qg, k_ctx).astype(jnp.float32) * scale
    n_win = wr * GRID_W
    s = jnp.concatenate([s_win.reshape(B, H, rows, GRID_W, n_win), s_ctx], axis=-1)
    p = jax.nn.softmax(s, axis=-1).astype(v.dtype)
    p_win = p[..., :n_win].reshape(B, H, rows, GRID_W, wr, GRID_W)
    o = jnp.einsum('bhrqwk,brwkhd->brqhd', p_win, vg) + jnp.einsum('bhrqk,bkhd->brqhd', p[..., n_win:], v_ctx)
    return o.reshape(B, T, H * d)

def hier_moe(h, router_group, router_expert, w_gate, w_up, w_down):
    B, T, D = h.shape
    ht = h.reshape(B * T, D)
    g_logits = (ht @ router_group).astype(jnp.float32)
    g_prob = jax.nn.softmax(g_logits, axis=-1)
    g_sel = jnp.argmax(g_logits, axis=-1)
    g_w = jnp.take_along_axis(g_prob, g_sel[:, None], axis=-1)
    e_logits = (ht @ router_expert).astype(jnp.float32).reshape(-1, N_GROUPS, EXPERTS_PER_GROUP)
    e_in = jnp.take_along_axis(e_logits, g_sel[:, None, None], axis=1)[:, 0]
    top_v, top_i = lax.top_k(e_in, TOP_K_IN_GROUP)
    top_w = jax.nn.softmax(top_v, axis=-1) * g_w
    expert_id = g_sel[:, None] * EXPERTS_PER_GROUP + top_i
    gates = jnp.sum(jax.nn.one_hot(expert_id, N_EXPERTS, dtype=jnp.float32) * top_w[..., None], axis=1).astype(h.dtype)
    a = jnp.einsum('nd,edf->nef', ht, w_gate)
    u = jnp.einsum('nd,edf->nef', ht, w_up)
    y = jnp.einsum('nef,efd->nd', jax.nn.silu(a) * u * gates[:, :, None], w_down)
    return y.reshape(B, T, D)

def merge_mixers(na_o, ret_o, ret_g, diff_o, p, lam_init):
    B, T = na_o.shape[:2]
    ret_o = head_layer_norm(ret_o).reshape(B, T, RET_W) * p['ret_gn_w'] + p['ret_gn_b']
    ret_o = ret_o * jax.nn.silu(ret_g)
    diff_o = head_rms_norm(diff_o).reshape(B, T, DIFF_W) * p['diff_norm_w'] * (1.0 - lam_init)
    mix = jnp.concatenate([na_o.reshape(B, T, NA_W), ret_o, diff_o], axis=-1)
    return mix @ p['w_out']

def post_norm_residual(x, y, gate, w, b):
    return layer_norm(ALPHA * x + gate * y, w, b)

def channel_sublayer(x, shift, scale, gate, p):
    h = x * (1 + scale) + shift
    y = hier_moe(h, p['router_group'], p['router_expert'], p['exp_w_gate'], p['exp_w_up'], p['exp_w_down'])
    return post_norm_residual(x, y, gate, p['ln2_w'], p['ln2_b'])

def context_layer(x, c_ctx, p, l):
    B, T = x.shape[:2]
    shift1, scale1, gate1, shift2, scale2, gate2 = modulation(c_ctx[None, :], p['w_mod'], p['b_mod'])
    h = x * (1 + scale1) + shift1
    na_q, na_k, na_v, ret_q, ret_k, ret_v, ret_g, diff_q, diff_k, diff_v = project(h, p['w_in'])
    na_o = dense_attn(na_q, na_k, na_v)
    zero = jnp.zeros((B, RET_HEADS, HEAD_DIM, HEAD_DIM), ret_q.dtype)
    ret_o, s_fwd, s_bwd = retention_bidir(ret_q, ret_k, ret_v, p['ret_decay'], zero, zero)
    lam_init = 0.8 - 0.6 * math.exp(-0.3 * l)
    diff_o = diff_attn(diff_q, diff_k, diff_v, diff_lambda_value(p['diff_lambda'], lam_init))
    y = merge_mixers(na_o, ret_o, ret_g, diff_o, p, lam_init)
    x = post_norm_residual(x, y, gate1, p['ln1_w'], p['ln1_b'])
    x = channel_sublayer(x, shift2, scale2, gate2, p)
    ret_state = jnp.stack([s_fwd, s_bwd], axis=1)
    return x, na_k, na_v, ret_state, diff_k.reshape(B, T, DIFF_HEADS, 2 * DIFF_D), diff_v

def latent_layer(x, c, na_k_ctx, na_v_ctx, ret_state, diff_k_ctx, diff_v_ctx, p, l):
    B, T = x.shape[:2]
    shift1, scale1, gate1, shift2, scale2, gate2 = modulation(c, p['w_mod'], p['b_mod'])
    h = x * (1 + scale1) + shift1
    na_q, na_k, na_v, ret_q, ret_k, ret_v, ret_g, diff_q, diff_k, diff_v = project(h, p['w_in'])
    na_o = na_latent(na_q, na_k, na_v, na_k_ctx, na_v_ctx, p['na_rel_bias'])
    s0 = ret_state.astype(ret_q.dtype)
    ret_o, _, _ = retention_bidir(ret_q, ret_k, ret_v, p['ret_decay'], s0[:, 0], s0[:, 1])
    t = jnp.arange(T)
    row, col = t // GRID_W, t % GRID_W
    q_r = axial_rope(diff_q, row, col)
    k_r = axial_rope(diff_k, row, col)
    k_all = jnp.concatenate([diff_k_ctx.reshape(B, diff_k_ctx.shape[1], DIFF_HEADS, 2, DIFF_D), k_r], axis=1)
    v_all = jnp.concatenate([diff_v_ctx, diff_v], axis=1)
    lam_init = 0.8 - 0.6 * math.exp(-0.3 * l)
    diff_o = diff_attn(q_r, k_all, v_all, diff_lambda_value(p['diff_lambda'], lam_init))
    y = merge_mixers(na_o, ret_o, ret_g, diff_o, p, lam_init)
    x = post_norm_residual(x, y, gate1, p['ln1_w'], p['ln1_b'])
    return channel_sublayer(x, shift2, scale2, gate2, p)

def setup_inputs(seed: int = 0) -> dict:
    key = jax.random.key(seed)
    keys = jax.random.split(key, 28)

    def nrm(i, shape, s):
        return jax.random.normal(keys[i], shape, jnp.float32) * s

    D = D_MODEL
    ret_base = jnp.asarray(np.log(2.0 ** (5 + np.arange(RET_HEADS)) - 1.0), dtype=jnp.float32)
    return {
        'x_prompt': nrm(0, (BATCH, SEQ, D), 1.0),
        'x_sample': nrm(1, (DEC_BATCH, DEC_SEQ, D), 1.0),
        'c': nrm(2, (DEC_BATCH, D), 1.0),
        'cache_na_k': nrm(3, (DEC_BATCH, DEPTH, PAST_LEN, NA_HEADS, HEAD_DIM), 1.0),
        'cache_na_v': nrm(4, (DEC_BATCH, DEPTH, PAST_LEN, NA_HEADS, HEAD_DIM), 1.0),
        'state_ret': nrm(5, (DEC_BATCH, DEPTH, 2, RET_HEADS, HEAD_DIM, HEAD_DIM), 1.0),
        'cache_diff_k': nrm(6, (DEC_BATCH, DEPTH, PAST_LEN, DIFF_HEADS, 2 * DIFF_D), 1.0),
        'cache_diff_v': nrm(7, (DEC_BATCH, DEPTH, PAST_LEN, DIFF_HEADS, DIFF_DV), 1.0),
        'c_ctx': nrm(8, (D,), 1.0),
        'w_mod': nrm(9, (DEPTH, D, 6 * D), 0.5 * D ** -0.5),
        'b_mod': nrm(10, (DEPTH, 6 * D), 0.01),
        'w_in': nrm(11, (DEPTH, D, IN_COLS), D ** -0.5),
        'na_rel_bias': nrm(12, (DEPTH, NA_HEADS, 2 * NA_WIN_ROWS - 1, 2 * NA_WIN_COLS - 1), 0.1),
        'ret_decay': jnp.broadcast_to(ret_base, (DEPTH, 2, RET_HEADS)) + nrm(13, (DEPTH, 2, RET_HEADS), 0.1),
        'ret_gn_w': 1.0 + nrm(14, (DEPTH, RET_W), 0.05),
        'ret_gn_b': nrm(15, (DEPTH, RET_W), 0.01),
        'diff_lambda': nrm(16, (DEPTH, 4, DIFF_D), 0.1),
        'diff_norm_w': 1.0 + nrm(17, (DEPTH, DIFF_W), 0.05),
        'w_out': nrm(18, (DEPTH, MIX_W, D), BETA * MIX_W ** -0.5),
        'ln1_w': 1.0 + nrm(19, (DEPTH, D), 0.05),
        'ln1_b': nrm(20, (DEPTH, D), 0.01),
        'router_group': nrm(21, (DEPTH, D, N_GROUPS), D ** -0.5),
        'router_expert': nrm(22, (DEPTH, D, N_EXPERTS), D ** -0.5),
        'exp_w_gate': nrm(23, (DEPTH, N_EXPERTS, D, EXPERT_FF), D ** -0.5),
        'exp_w_up': nrm(24, (DEPTH, N_EXPERTS, D, EXPERT_FF), D ** -0.5),
        'exp_w_down': nrm(25, (DEPTH, N_EXPERTS, EXPERT_FF, D), BETA * EXPERT_FF ** -0.5),
        'ln2_w': 1.0 + nrm(26, (DEPTH, D), 0.05),
        'ln2_b': nrm(27, (DEPTH, D), 0.01),
    }

def reference(x_prompt, x_sample, c, cache_na_k, cache_na_v, state_ret, cache_diff_k, cache_diff_v, c_ctx,
              w_mod, b_mod, w_in, na_rel_bias, ret_decay, ret_gn_w, ret_gn_b, diff_lambda, diff_norm_w, w_out,
              ln1_w, ln1_b, router_group, router_expert, exp_w_gate, exp_w_up, exp_w_down, ln2_w, ln2_b):
    y_prompt = x_prompt
    y_sample = x_sample
    na_ks, na_vs, ret_states, diff_ks, diff_vs = [], [], [], [], []
    for l in range(DEPTH):
        p = dict(w_mod=w_mod[l], b_mod=b_mod[l], w_in=w_in[l], na_rel_bias=na_rel_bias[l],
                 ret_decay=ret_decay[l], ret_gn_w=ret_gn_w[l], ret_gn_b=ret_gn_b[l],
                 diff_lambda=diff_lambda[l], diff_norm_w=diff_norm_w[l], w_out=w_out[l],
                 ln1_w=ln1_w[l], ln1_b=ln1_b[l], router_group=router_group[l], router_expert=router_expert[l],
                 exp_w_gate=exp_w_gate[l], exp_w_up=exp_w_up[l], exp_w_down=exp_w_down[l],
                 ln2_w=ln2_w[l], ln2_b=ln2_b[l])
        y_prompt, nk, nv, rs, dk, dv = context_layer(y_prompt, c_ctx, p, l)
        na_ks.append(nk)
        na_vs.append(nv)
        ret_states.append(rs)
        diff_ks.append(dk)
        diff_vs.append(dv)
        y_sample = latent_layer(y_sample, c, cache_na_k[:, l], cache_na_v[:, l], state_ret[:, l],
                                cache_diff_k[:, l], cache_diff_v[:, l], p, l)
    new_na_k = jnp.stack(na_ks, axis=1)
    new_na_v = jnp.stack(na_vs, axis=1)
    new_ret_state = jnp.stack(ret_states, axis=1)
    new_diff_k = jnp.stack(diff_ks, axis=1)
    new_diff_v = jnp.stack(diff_vs, axis=1)
    return (y_prompt, y_sample, new_na_k, new_na_v, new_ret_state, new_diff_k, new_diff_v)


_drawn_inputs = setup_inputs


def setup_inputs(seed=0):
    import zlib

    import numpy as np

    out = dict(_drawn_inputs(seed))
    spreads = {}
    factors = {'cache_na_k': 6.6,
     'cache_na_v': 5.293,
     'cache_diff_k': 3.634,
     'cache_diff_v': 3.328,
     'na_rel_bias': 64.0,
     'ret_gn_w': 8.0,
     'ret_gn_b': 64.0,
     'diff_lambda': 8.0,
     'diff_norm_w': 8.0,
     'ln1_b': 2.796}
    for name, (base, spread) in spreads.items():
        noise = np.random.default_rng([zlib.crc32(name.encode()), seed]).standard_normal(out[name].shape)
        drawn = base * np.exp(spread * noise) if base else spread * noise
        out[name] = __import__('jax').numpy.asarray(drawn.astype(out[name].dtype))
    for name, factor in factors.items():
        out[name] = (out[name] * factor).astype(out[name].dtype)
    return out
```

```python
import math
from contextlib import ExitStack

import numpy as np

import concourse.bass as bass
from concourse import mybir

F32 = mybir.dt.float32
I32 = mybir.dt.int32
U32 = mybir.dt.uint32
ALU = mybir.AluOpType
ACT = mybir.ActivationFunctionType
AX = mybir.AxisListType

P = 128
D = 1024
DEPTH = 2
CTX = 128
LAT = 256
TOKENS = CTX + LAT
TILES = TOKENS // P
CH = D // P
GRID_W = 64
HD = 64
NA_HEADS = 6
WIN_ROWS = 8
WIN_COLS = 16
RET_HEADS = 6
DIFF_HEADS = 4
DIFF_D = 32
NA_W = NA_HEADS * HD
RET_W = RET_HEADS * HD
DIFF_W = DIFF_HEADS * HD
IN_COLS = 3 * NA_W + 4 * RET_W + 3 * DIFF_W
GROUPS = 4
PER_GROUP = 8
EXPERTS = GROUPS * PER_GROUP
FF = 256
ROPE_BASE = 10000.0
LN_EPS = 1e-5
NEG_INF = -1e30
ALPHA = (2.0 * DEPTH) ** 0.25
NA_SCALE = HD ** -0.5
RET_SCALE = HD ** -0.5
DIFF_SCALE = DIFF_D ** -0.5

SLOTS = 64
ROUNDS_MAX = TOKENS // SLOTS
TRIPS_MAX = ROUNDS_MAX * GROUPS
PAIRS = PER_GROUP // 2
ROWS = 1 + 2 * TOKENS

RING = 12
UNIT = 2048
UCOL = UNIT // CH
MOD_UNITS = 6 * D // UCOL
IN_UNITS = -(-IN_COLS // UCOL)
OUT_UNITS = D // UCOL
STATIC_UNITS = MOD_UNITS + IN_UNITS + OUT_UNITS
STATIC_SPAN = -(-STATIC_UNITS // RING) * RING
TRIP_UNITS = 3 * PER_GROUP
SLOT_USES = [len(range(s, STATIC_UNITS, RING)) for s in range(RING)]

WORK = 0
HT = 0
NQT = 3072
NKT = NQT + 3 * TOKENS
RQT = NKT + 3 * 512
RKT = RQT + 3 * TOKENS
DQT = RKT + 3 * TOKENS
DKT = DQT + 2 * TOKENS
MODROW = DQT
ROPE_T = DQT
PN = DKT + 2 * 512
PN_W = 2304
NKC = PN + 3 * PN_W
ARENA = NKC + NA_W
C_NV, C_RK, C_RV, C_RG, C_DQ, C_DK, C_DV = 0, 384, 768, 1152, 1536, 1792, 2048
C_NAO, C_RETO, C_DIFFO = C_DQ, C_RK, C_RV
MIXT = 3072
LNW, LNB, GATE = 0, 1024, 2048
Z, S2, T2 = 6144, 7168, 8192
H2, H2T, XG = 3072, 10240, 6144
GSEL, HIDDEN, YB = 1536, 0, 13312
ROUTE = 15360
GATH = 3072

K_ID, K_TRI, K_ONE, K_A, K_B = 0, 128, 256, 384, 512
K_IOTA = 640
K_COS = K_IOTA + SLOTS
K_SIN = K_COS + 64
K_IP1 = K_SIN + 64
K_128I = K_IP1 + 1
K_127J = K_128I + 1
K_J = K_127J + 1
K_SEL = K_J + 1
K_TB4 = K_SEL + 2
K_TB32 = K_TB4 + GROUPS
K_ROW = K_TB32 + EXPERTS
K_EMPTY = K_ROW + TILES
K_THR = K_EMPTY + 1
K_MHALF = K_THR + ROUNDS_MAX
K_COLS = K_MHALF + 3


def shape_constants():
    k = np.zeros((P, K_COLS), np.float32)
    i = np.arange(P)
    k[:, K_ID:K_ID + P] = np.eye(P)
    k[:, K_TRI:K_TRI + P] = i[:, None] < i[None, :]
    k[:, K_ONE:K_ONE + P] = 1.0
    k[:, K_A:K_A + P] = np.maximum(i[None, :] - i[:, None], 0)
    k[:, K_B:K_B + P] = np.maximum(i[:, None] - i[None, :], 0)
    k[:, K_IOTA:K_IOTA + SLOTS] = np.arange(SLOTS)
    n = DIFF_D // 4
    freq = (np.float32(ROPE_BASE) ** (-np.arange(n, dtype=np.float32) / n)).astype(np.float32)
    for t in range(2):
        pos = np.arange(t * P, (t + 1) * P)
        for a, at in enumerate((pos // GRID_W, pos % GRID_W)):
            ang = at.astype(np.float32)[:, None] * freq[None, :]
            for x in range(2):
                c = 32 * t + 16 * a + 8 * x
                k[:, K_COS + c:K_COS + c + n] = np.cos(ang)
                k[:, K_SIN + c:K_SIN + c + n] = np.sin(ang) * (1 if x else -1)
    k[:, K_IP1] = i + 1
    k[:, K_128I] = P - i
    k[:, K_127J] = P - 1 - i
    k[:, K_J] = i
    for j in range(4):
        k[32 * j, K_SEL] = 1
        k[32 * j + 1, K_SEL + 1] = 1
    k[:, K_TB4:K_TB4 + GROUPS] = GROUPS - np.arange(GROUPS)
    k[:, K_TB32:K_TB32 + EXPERTS] = EXPERTS - np.arange(EXPERTS)
    for t in range(TILES):
        k[:, K_ROW + t] = 2 * (t * P + i) + 1
    k[:, K_EMPTY] = 2 * ROWS + i
    k[:, K_THR:K_THR + ROUNDS_MAX] = SLOTS * np.arange(ROUNDS_MAX)
    k[:, K_THR] = -1
    k[:, K_MHALF] = -0.5
    return k


def layer_constants():
    lam = [0.8 - 0.6 * math.exp(-0.3 * l) for l in range(DEPTH)]
    return np.array([[v, 1.0 - v] for v in lam], np.float32)


def stage_order():
    order = [("mod", q) for q in range(4)] + [("col", 0)]
    order += [("mod", q) for q in range(4, 8)] + [("col", 1), ("xT", 0)]
    q, due = 8, None
    for u in range(IN_UNITS):
        order.append(("win", u))
        if due is not None:
            order.append(("col", due))
            due = None
        for _ in range(2 if u < 5 else 1):
            if q < MOD_UNITS:
                order.append(("mod", q))
                if q % 4 == 3:
                    due = q // 4
                q += 1
                if due is not None:
                    break
    assert q == MOD_UNITS and due is None
    return order


ORDER = stage_order()
assert [x for x in ORDER if x[0] == "col"][-1] == ("col", 5) and ORDER.index(("col", 5)) < ORDER.index(("win", 12))
STATIC = [x for x in ORDER if x[0] in ("mod", "win")] + [("wout", u) for u in range(OUT_UNITS)]
UNIT_OF = {x: n for n, x in enumerate(STATIC)}
assert len(STATIC) == STATIC_UNITS


def bank_jobs():
    jobs = [("xT", c, 0) for c in range(CH)]
    for u in range(IN_UNITS):
        for cb in (2 * u, 2 * u + 1):
            if cb <= 5 or 9 <= cb <= 11:
                jobs.append(("pT", cb, u))
        wide = [cb for cb in (2 * u, 2 * u + 1) if (6 <= cb <= 8 or cb >= 12) and cb < IN_COLS // P]
        if wide:
            jobs += [("pN", tuple(wide), (u, t)) for t in range(TILES)]
    jobs += [("nkc", 0, 0), ("ck", 0, 0), ("cdk", 0, 0)]
    jobs += [("rkT", b, 0) for b in range(3)]
    jobs += [("dqT", b, 0) for b in range(2)] + [("dkT", b, 0) for b in range(2)]
    return jobs


JOBS = bank_jobs()
DRAIN = [("act", "dve")[n % 2] for n in range(len(JOBS))]
DRAINED = {e: [sum(d == e for d in DRAIN[:n + 1]) for n in range(len(JOBS))] for e in ("act", "dve")}
JOB_BANKS = 5
LAST_JOB = {}
for _n, _k in enumerate(JOBS):
    if _k[0] == "pT":
        LAST_JOB[_k[2]] = _n
    if _k[0] == "pN":
        LAST_JOB[_k[2][0]] = _n
FIRST_EXTRA = next(n for n, k in enumerate(JOBS) if k[0] == "nkc")

ATT = [("diff", t, h) for t in (1, 2, 0) for h in range(DIFF_HEADS)]
N_DIFF = len(ATT)
ATT += [("na", t, h) for t in (1, 2, 0) for h in range(NA_HEADS)]
N_ATT = len(ATT)
RET_NORM_AT = 6
DIFF_NORM_AT = N_DIFF + 3


def keys_of(tile):
    return P if tile == 0 else LAT + P


def col_of_block(cb):
    return (cb - 6) * P if cb <= 8 else C_RK + (cb - 12) * P


class Signal:

    def __init__(self, sem, step, start):
        self.sem, self.step, self.start = sem, step, start

    def at(self, i, k):
        return i * self.step + (k + self.start)


class Chain:

    def __init__(self, eng, signal, i):
        self.eng, self.links, self.i, self.n = eng, signal, i, 0

    def link(self, ins, wait=lambda eng, signal, value: eng.wait_ge(signal.sem, value)):
        self.n += 1
        ins.then_inc(self.links.sem, 1)
        wait(self.eng, self.links, self.links.at(self.i, self.n))


def build(nc, x_prompt, x_sample, c, cache_na_k, cache_na_v, state_ret, cache_diff_k, cache_diff_v, c_ctx,
          w_mod, b_mod, w_in, na_rel_bias, ret_decay, ret_gn_w, ret_gn_b, diff_lambda, diff_norm_w, w_out,
          ln1_w, ln1_b, router_group, router_expert, exp_w_gate, exp_w_up, exp_w_down, ln2_w, ln2_b,
          shape_k, layer_k,
          y_prompt, y_sample, new_na_k, new_na_v, new_ret_state, new_diff_k, new_diff_v):
    rows = nc.dram_tensor("expert_rows", (ROWS, D), F32).ap()

    toeplitz = nc.dram_tensor("toeplitz", (DEPTH, 2, GRID_W, NA_HEADS * 6 * GRID_W), F32).ap()

    with ExitStack() as ctx:
        def sb(name, shape, dt=F32):
            return ctx.enter_context(nc.sbuf_tensor(name, shape, dt))

        def signal(name, step=0, start=0):
            s = Signal(ctx.enter_context(nc.semaphore(name)), step, start)
            if start:
                started.append(s)
            return s

        started = []

        ring = sb("ring", [P, RING, UNIT])
        arena = sb("arena", [P, ARENA])
        x = sb("x", [P, TILES, D])
        kc = sb("kc", [P, K_COLS])
        cond = sb("cond", [P, CH, 32])
        condraw = sb("condraw", [P, 2, CH])
        modc = sb("modc", [P, 6, CH, 2])
        na_kc = sb("na_kc", [P, NA_W])
        na_vc = sb("na_vc", [P, NA_W])
        df_kc = sb("df_kc", [P, DIFF_W])
        df_vc = sb("df_vc", [P, DIFF_W])
        s0 = sb("s0", [P, 2, 3, HD])
        bias = sb("bias", [P, NA_HEADS, 6, GRID_W])
        gnw = sb("gnw", [P, RET_W])
        gnb = sb("gnb", [P, RET_W])
        dnw = sb("dnw", [P, DIFF_W])
        lamp = sb("lamp", [P, 4, DIFF_D])
        dec = sb("dec", [P, 2, RET_HEADS])
        bmod = sb("bmod", [P, 6, CH])
        rw = sb("rw", [P, CH, GROUPS + EXPERTS])
        lamk = sb("lamk", [P, 2])
        decay = sb("decay", [P, RET_HEADS, P])
        lg = sb("lg", [P, 4, 2, RET_HEADS])
        qdec = sb("qdec", [P, 2, RET_HEADS])
        kdec = sb("kdec", [P, 2, RET_HEADS])
        cdec = sb("cdec", [P, 2, 3])
        lam = sb("lam", [P, 8])
        stats = sb("stats", [P, N_ATT, 6])
        lamt = sb("lamt", [P, 2, DIFF_D])
        diff_s = sb("diff_s", [P, 3, TILES * DIFF_HEADS])
        norm_s = sb("norm_s", [P, 4, TILES * RET_HEADS])
        ln_s = sb("ln_s", [P, TILES, 20])
        rounds = sb("rounds", [1, 4], I32)
        trips = sb("trips", [1, DEPTH * TRIPS_MAX + 1], I32)
        ps = ctx.enter_context(nc.psum_tensor("ps", [P, 8, 512], F32))

        ident = kc[:, K_ID:K_ID + P]
        ones = kc[:, K_ONE:K_ONE + P]

        def at(base, *dims):
            n = math.prod(dims)
            v = arena[:, base:base + n]
            if len(dims) == 2:
                return v.rearrange("p (a b) -> p a b", a=dims[0])
            if len(dims) == 3:
                return v.rearrange("p (a b c) -> p a b c", a=dims[0], b=dims[1])
            return v

        hT = at(HT, CH, TOKENS)
        nqT, nkT = at(NQT, 3, TOKENS), at(NKT, 3, 512)
        rqT, rkT = at(RQT, 3, TOKENS), at(RKT, 3, TOKENS)
        dqT, dkT = at(DQT, 2, TOKENS), at(DKT, 2, 512)
        modrow = at(MODROW, D)
        pn = at(PN, TILES, PN_W)
        nkc = at(NKC, NA_W)
        kx = at(WORK, 4, RET_W)
        scb = [at(WORK + 1536, RET_HEADS, P), at(WORK + 768, RET_HEADS, P)]
        rt = at(WORK, 2, RET_W)
        snew = at(WORK + 2304, 2, 3, HD)
        sctx = at(WORK + 2688, 2, 3, HD)
        eb = [at(WORK + 768 * i, 2, TOKENS) for i in range(2)]
        pTb = [at(WORK + 1536 + TOKENS * i, 3, P) for i in range(2)]
        sq = at(WORK + 2304, 768)
        mixT = at(MIXT, CH, TOKENS)
        lnw, lnb, gate = at(LNW, D), at(LNB, D), at(GATE, D)
        z, s2, t2 = at(Z, D), at(S2, D), at(T2, D)
        h2, h2T = at(H2, TILES, D), at(H2T, CH, TOKENS)
        xg = at(XG, CH, PER_GROUP * SLOTS)
        gsel = at(GSEL, TILES, PER_GROUP, SLOTS)
        sil = [at(HIDDEN + FF * i, FF) for i in range(2)]
        hid = [at(HIDDEN + 2 * FF + FF * i, FF) for i in range(2)]
        hidT = [at(HIDDEN + 4 * FF + FF * i, 2, P) for i in range(2)]
        yb = [at(YB + D * i, D) for i in range(2)]
        gath = at(GATH, TILES, 2, D)

        def route(n, *dims):
            v = at(ROUTE + route.used, *dims)
            route.used += math.prod(dims)
            assert ROUTE + route.used <= ARENA
            return v
        route.used = 0
        wts = route(2, 2, TILES)
        rowid = route(TILES, TILES, EXPERTS)
        idxf = route(4, PAIRS)
        idxu = route(4, PAIRS).bitcast(U32)
        logit = route(0, TILES, GROUPS + EXPERTS)
        gst = route(0, 8, TILES)
        goh = route(0, TILES, GROUPS)
        gtmp = route(0, TILES, GROUPS)
        em = route(0, TILES, EXPERTS)
        et = route(0, TILES, EXPERTS)
        oh = route(0, 2, TILES, EXPERTS)
        mcount = route(0, TILES, EXPERTS)
        rankm = route(0, TILES, EXPERTS)
        cmpn = route(0, GROUPS + ROUNDS_MAX + 2)
        counts = route(0, ROUNDS_MAX, GROUPS)
        iotar = route(0, SLOTS)

        ring_full = [signal(f"ring_full{s}") for s in range(RING)]
        const_in = signal("const_in")
        toeplitz_out = signal("toeplitz_out")
        x_in = signal("x_in")
        N_SMALL = 19
        small_in = signal("small_in", 16 * N_SMALL)
        ln1_in, ln2_in = signal("ln1_in", 32), signal("ln2_in", 32)
        results_out = signal("results_out", 16 * 6)
        rows_out, rows_stored = signal("rows_out", 16 * PAIRS), signal("rows_stored", PAIRS, start=1)
        y_out = signal("y_out")
        gathered = [signal(f"gathered{i}", 16) for i in range(TILES)]
        cond_zero, cond_ready = signal("cond_zero"), signal("cond_ready")
        mod_ready, mod_copied = signal("mod_ready", MOD_UNITS), signal("mod_copied", MOD_UNITS)
        col_ready, modc_ready = signal("col_ready", 6), signal("modc_ready", 6)
        bc_ready, bc_copied = signal("bc_ready", 8), signal("bc_copied", 8, start=1)
        job_ready = signal("job_ready", len(JOBS))
        job_act = signal("job_act", DRAINED["act"][-1])
        job_dve = signal("job_dve", DRAINED["dve"][-1])
        rope_done = signal("rope_done", 1)
        bias_masked = signal("bias_masked", 4)
        lg_a, lg_b, lg_c = signal("decay_abs", 1), signal("decay_soft", 2), signal("decay_log", 1)
        dec_exponent, tables_ready = signal("dec_exponent", 1), signal("tables_ready", 9)
        kdec_scaled = signal("kdec_scaled", 1)
        lam_dot = signal("lam_dot", 1)
        lam_exp, lam_ready = signal("lam_exp", 1), signal("lam_ready", 1)
        swish_ready = signal("swish_ready", 3)
        kx_ready = signal("kx_ready", 1)
        state_ready, state_done = signal("state_ready", 1), signal("state_done", 1)
        sct_ready, sc_ready = signal("sct_ready", 3), signal("sc_ready", 3)
        ret_ready, ret_done = signal("ret_ready", 3), signal("ret_done", 3)
        ret_var, ret_normed = signal("ret_var", 1), signal("ret_normed", 1)
        diff_var, diff_normed = signal("diff_var", 1), signal("diff_normed", 1)
        scores_ready, negmax_ready = signal("scores_ready", N_ATT), signal("negmax_ready", N_ATT)
        exp_done, diffs_ready = signal("exp_done", N_ATT), signal("diffs_ready", N_DIFF)
        probsT_ready, probsT_copied = signal("probsT_ready", N_ATT), signal("probsT_copied", N_ATT)
        head_ready, head_done = signal("head_ready", N_ATT), signal("head_done", N_ATT)
        mixT_ready = signal("mixT_ready", CH)
        mixT_act, mixT_dve = signal("mixT_act", CH // 2), signal("mixT_dve", CH // 2)
        y_ready = signal("y_ready", OUT_UNITS)
        gated = signal("gated", TILES)
        var1, rstd1 = signal("var1", TILES), signal("rstd1", TILES)
        ln1_done, h2_ready = signal("ln1_done", TILES), signal("h2_ready", TILES)
        h2T_ready = signal("h2T_ready", CH)
        h2T_act, h2T_dve = signal("h2T_act", CH // 2), signal("h2T_dve", CH // 2)
        logits_ready = signal("logits_ready", 1, start=1)
        gexp_in, gexp_done = signal("gexp_in", 2), signal("gexp_done", 2)
        chosen, ranks_ready, routed = signal("chosen", 1), signal("ranks_ready", 1), signal("routed", 1)
        rounds_known = signal("rounds_known", 1)
        idx_ready, idx_known = signal("idx_ready", 1), signal("idx_known", 1, start=1)
        idx_link = signal("idx_link", 1)
        gsel_ready, xg_ready = signal("gsel_ready", 1), signal("xg_ready", CH, start=1)
        xg_act, xg_dve = signal("xg_act", CH // 2), signal("xg_dve", CH // 2)
        gate_ready, up_ready = signal("gate_ready", PAIRS, start=1), signal("up_ready", PAIRS, start=1)
        silu_done, hid_ready = signal("silu_done", PAIRS), signal("hid_ready", PAIRS, start=1)
        hidT_ready, hidT_copied = signal("hidT_ready", PAIRS), signal("hidT_copied", PAIRS, start=1)
        down_ready = signal("down_ready", PAIRS, start=1)
        row_act, row_dve = signal("row_act", PAIRS, start=1), signal("row_dve", PAIRS, start=1)
        var2, rstd2, ln2_done = signal("var2", TILES), signal("rstd2", TILES), signal("ln2_done", TILES, start=1)
        combined = signal("combined", TILES, start=1)
        dve_link = signal("dve_link", DVE_LINKS)
        pool_link = signal("pool_link", POOL_LINKS)
        trip_link = signal("trip_link", 1)
        passed = signal("passed")

        block = ctx.enter_context(nc.Block())

        def trips_before(eng, l, k=0):
            return eng.value_load(trips[0:1, bass.ds(l * TRIPS_MAX + k, 1)], min_val=0, max_val=DEPTH * TRIPS_MAX)

        def rounds_before(eng, l):
            return eng.value_load(rounds[0:1, bass.ds(l, 1)], min_val=0, max_val=DEPTH * ROUNDS_MAX)

        def trips_of(eng, l, r0, r, g):
            rel = nc.s_assert_within(r - r0, 0, ROUNDS_MAX - 1,
                                     skip_runtime_bounds_check_because="r runs from r0, at most ROUNDS_MAX further")
            k = rel * GROUPS + g
            return trips_before(eng, l, k), trips_before(eng, l, k + 1)

        def wait_alone(eng, signal, value):
            eng.wait_ge(signal.sem, value)
            eng.sem_inc(passed.sem, 1)

        def rounds_after(eng, l):
            wait_alone(eng, rounds_known, rounds_known.at(l, 1))
            return rounds_before(eng, l + 1)

        def full_static(eng, l, t0, n):
            s = n % RING
            eng.wait_ge(ring_full[s].sem, l * (16 * SLOT_USES[s]) + t0 * 32 + 16 * (n // RING + 1))

        def full_trip(eng, l, t, m):
            s = m % RING
            eng.wait_ge(ring_full[s].sem, l * (16 * SLOT_USES[s]) + t * 32 + 16 * (SLOT_USES[s] + m // RING + 1))

        def wait_released(eng, l, n):
            kind, i = STATIC[n]
            if kind == "mod":
                eng.wait_ge(mod_ready.sem, mod_ready.at(l, i + 1))
            elif kind == "win":
                eng.wait_ge(job_ready.sem, job_ready.at(l, LAST_JOB[i] + 1))
            else:
                eng.wait_ge(y_ready.sem, y_ready.at(l, i + 1))

        @block.sync
        def _(sp):
            for s in started:
                sp.sem_inc(s.sem, 1)
            sp.dma_start(condraw[:, 0, :], c_ctx.rearrange("(p c) -> p c", p=P)).then_inc(const_in.sem, 16)
            sp.dma_start(condraw[:, 1, :], c.rearrange("o (p c) -> p (o c)", p=P)).then_inc(const_in.sem, 16)
            sp.dma_start(kc[:, :], shape_k).then_inc(const_in.sem, 16)
            sp.dma_start(x[:, 0, :], x_prompt.rearrange("o p d -> (o p) d")).then_inc(x_in.sem, 16)
            sp.dma_start(x[:, 1:3, :], x_sample.rearrange("o (t p) d -> p (o t) d", p=P)).then_inc(x_in.sem, 16)

            def small_loads(l):
                n = [0]

                def load(dst, src):
                    n[0] += 1
                    sp.dma_start(dst, src).then_inc(small_in.sem, 16)

                one = bass.ds(l, 1)
                load(bmod[:, :, :], b_mod[one].rearrange("o (s p c) -> p (o s) c", s=6, p=P))
                load(dec[:, :, :], ret_decay[one].rearrange("o a h -> o (a h)").to_broadcast([P, 2 * RET_HEADS]).rearrange("p (a h) -> p a h", a=2))
                load(lamp[:, :, :], diff_lambda[one].rearrange("o a h -> o (a h)").to_broadcast([P, 4 * DIFF_D]).rearrange("p (a h) -> p a h", a=4))
                load(lamk[:, :], layer_k[one].to_broadcast([P, 2]))
                load(gnw[:, :], ret_gn_w[one].to_broadcast([P, RET_W]))
                load(gnb[:, :], ret_gn_b[one].to_broadcast([P, RET_W]))
                load(dnw[:, :], diff_norm_w[one].to_broadcast([P, DIFF_W]))
                load(na_kc[:, :], cache_na_k[0, one].rearrange("o p h d -> (o p) (h d)"))
                load(na_vc[:, :], cache_na_v[0, one].rearrange("o p h d -> (o p) (h d)"))
                load(df_kc[:, :], cache_diff_k[0, one].rearrange("o p h d -> (o p) (h d)"))
                load(df_vc[:, :], cache_diff_v[0, one].rearrange("o p h d -> (o p) (h d)"))
                load(rw[:, :, 0:GROUPS], router_group[one].rearrange("o (p c) e -> p (o c) e", p=P))
                load(rw[:, :, GROUPS:], router_expert[one].rearrange("o (p c) e -> p (o c) e", p=P))
                for half in range(2):
                    for a in range(2):
                        load(s0[64 * half:64 * half + 64, a, :, :],
                             state_ret[0, one, a, half::2].rearrange("o h k v -> k (o h) v"))
                for half in range(2):
                    load(bias[64 * half:64 * half + 64, :, :, :].rearrange("p h r c -> p (h r c)"),
                         toeplitz[one, half].rearrange("o p n -> (o p) n"))
                assert n[0] == N_SMALL, n

            def load_static(l, t0, n):
                kind, i = STATIC[n]
                s = n % RING
                if n >= RING:
                    wait_released(sp, l, n - RING)
                dst = ring[:, s, :].rearrange("p (c n) -> p c n", c=CH)
                one = bass.ds(l, 1)
                if kind == "mod":
                    src = w_mod[one, :, i * UCOL:(i + 1) * UCOL].rearrange("o (p c) n -> p (o c) n", p=P)
                elif kind == "win":
                    w = min(UCOL, IN_COLS - i * UCOL)
                    dst = dst[:, :, 0:w]
                    src = w_in[one, :, i * UCOL:i * UCOL + w].rearrange("o (p c) n -> p (o c) n", p=P)
                else:
                    src = w_out[one, :, i * UCOL:(i + 1) * UCOL].rearrange("o (c p) n -> p (o c) n", p=P)
                sp.dma_start(dst, src).then_inc(ring_full[s].sem, 16)

            def load_experts(l, t, g, first):
                for m in range(TRIP_UNITS):
                    pair, kind, which = m // 6, (m % 6) // 2, m % 2
                    s = m % RING
                    if first and m < RING:
                        n = STATIC_SPAN - RING + m
                        wait_released(sp, l, n if n < STATIC_UNITS else n - RING)
                    else:
                        before = (gate_ready, up_ready, down_ready)[kind]
                        sp.wait_ge(before.sem, before.at(t, pair - 1))
                    e = g * PER_GROUP + (2 * pair + which)
                    w = (exp_w_gate, exp_w_up, exp_w_down)[kind]
                    src = w.rearrange("l e (p c) n -> (l e) p (c n)", p=P)[bass.ds(l * EXPERTS + e, 1)]
                    sp.dma_start(ring[:, s, :], src.rearrange("o p n -> (o p) n")).then_inc(ring_full[s].sem, 16)

            sp.wait_ge(cond_zero.sem, 3)
            sp.wait_ge(toeplitz_out.sem, 16 * 2 * DEPTH * NA_HEADS)
            with sp.Fori(0, DEPTH) as l:
                t0 = trips_before(sp, l)
                sp.wait_ge(down_ready.sem, down_ready.at(t0, 0))
                for n in range(RING):
                    load_static(l, t0, n)
                sp.wait_ge(logits_ready.sem, logits_ready.at(l, 0))
                small_loads(l)
                for n in range(RING, STATIC_UNITS):
                    load_static(l, t0, n)
                load_experts(l, t0, 0, True)
                with sp.Fori(1, GROUPS) as g:
                    load_experts(l, t0 + g, g, False)
                r1 = rounds_after(sp, l)
                r0 = rounds_before(sp, l)
                with sp.If(r1 > r0 + 1):
                    with sp.Fori(r0 + 1, r1) as r:
                        with sp.Fori(0, GROUPS) as g:
                            t, after = trips_of(sp, l, r0, r, g)
                            with sp.If(after > t):
                                load_experts(l, t, g, False)
            sp.wait_ge(ln2_done.sem, ln2_done.at(DEPTH - 1, TILES))
            sp.dma_start(y_prompt.rearrange("o p d -> (o p) d"), x[:, 0, :]).then_inc(y_out.sem, 16)
            sp.dma_start(y_sample.rearrange("o (t p) d -> p (o t) d", p=P), x[:, 1:3, :]).then_inc(y_out.sem, 16)
            sp.wait_ge(y_out.sem, 32)
            sp.wait_ge(results_out.sem, DEPTH * results_out.step)

        @block.tensor
        def _(pe):
            pe.wait_ge(const_in.sem, 48)
            pe.wait_ge(cond_zero.sem, 3)
            pe.wait_ge(cond_ready.sem, 1)

            def unit(n):
                return ring[:, n % RING, :].rearrange("p (c n) -> p c n", c=CH)

            def bank_free(l, j):
                if j >= JOB_BANKS:
                    k = j - JOB_BANKS
                    done = job_act if DRAIN[k] == "act" else job_dve
                    pe.wait_ge(done.sem, done.at(l, DRAINED[DRAIN[k]][k]))

            def broadcast(l, n, s, k):
                if n:
                    pe.wait_ge(bc_copied.sem, bc_copied.at(l, n))
                for ch in range(CH):
                    mm = pe.matmul(ps[:, 6 + ch // 4, (ch % 4) * P:(ch % 4 + 1) * P],
                                   modc[:, s, ch, k:k + 1].to_broadcast([P, P]), ident, start=True, stop=True)
                mm.then_inc(bc_ready.sem, 1)

            def mod_unit(l, t0, q):
                n = UNIT_OF["mod", q]
                full_static(pe, l, t0, n)
                if q >= 2:
                    pe.wait_ge(mod_copied.sem, mod_copied.at(l, q - 1))
                for ch in range(CH):
                    j = ch % 4
                    mm = pe.matmul(ps[32 * j:32 * j + 32, q % 2, 0:UCOL], cond[:, ch, :], unit(n)[:, ch, :],
                                   start=(ch < 4), stop=(ch >= 4))
                mm.then_inc(mod_ready.sem, 1)

            def mod_cols(l, s):
                pe.wait_ge(mod_copied.sem, mod_copied.at(l, 4 * (s + 1)))
                if s:
                    pe.wait_ge(modc_ready.sem, modc_ready.at(l, s))
                for ch in range(CH):
                    at2 = (s * CH + ch) * 2
                    mm = pe.matmul(ps[:, 2, at2:at2 + 2], modrow[:, ch::CH], kc[:, K_SEL:K_SEL + 2],
                                   start=True, stop=True)
                mm.then_inc(col_ready.sem, 1)

            def tokens_T(l):
                for ch in range(CH):
                    bank_free(l, ch)
                    for t in range(TILES):
                        mm = pe.transpose(ps[:, 3 + ch % JOB_BANKS, t * P:(t + 1) * P], x[:, t, ch::CH], ident)
                    mm.then_inc(job_ready.sem, 1)

            def project(l, t0, u):
                n = UNIT_OF["win", u]
                full_static(pe, l, t0, n)
                if u == 0:
                    pe.wait_ge(job_act.sem, job_act.at(l, CH // 2))
                    pe.wait_ge(job_dve.sem, job_dve.at(l, CH // 2))
                for j, (kind, what, where) in enumerate(JOBS):
                    bank = 3 + j % JOB_BANKS
                    if kind == "pT" and where == u:
                        bank_free(l, j)
                        w = unit(n)[:, :, (what % 2) * P:(what % 2 + 1) * P]
                        for ch in range(CH):
                            mm = pe.matmul(ps[:, bank, 0:TOKENS], w[:, ch, :], hT[:, ch, :],
                                           start=(ch == 0), stop=(ch == CH - 1))
                        mm.then_inc(job_ready.sem, 1)
                    elif kind == "pN" and where[0] == u:
                        bank_free(l, j)
                        t, a, b = where[1], what[0] % 2, what[-1] % 2 + 1
                        for ch in range(CH):
                            mm = pe.matmul(ps[:, bank, 0:(b - a) * P], hT[:, ch, t * P:(t + 1) * P],
                                           unit(n)[:, ch, a * P:b * P], start=(ch == 0), stop=(ch == CH - 1))
                        mm.then_inc(job_ready.sem, 1)

            def turns(l):
                pe.wait_ge(small_in.sem, small_in.at(l, small_in.step))
                for j, (kind, b, _) in enumerate(JOBS[FIRST_EXTRA:], FIRST_EXTRA):
                    bank_free(l, j)
                    if j == FIRST_EXTRA:
                        pe.wait_ge(job_act.sem, job_act.at(l, DRAINED["act"][j - 1]))
                        pe.wait_ge(job_dve.sem, job_dve.at(l, DRAINED["dve"][j - 1]))
                    if kind == "dqT" and b == 0:
                        pe.wait_ge(rope_done.sem, rope_done.at(l, 1))
                    if kind == "nkc":
                        parts = [nkT[:, i, 0:P] for i in range(3)]
                    elif kind in ("ck", "cdk"):
                        cache = na_kc if kind == "ck" else df_kc
                        parts = [cache[:, i * P:(i + 1) * P] for i in range(3 if kind == "ck" else 2)]
                    else:
                        c0 = {"rkT": C_RK, "dqT": C_DQ, "dkT": C_DK}[kind] + b * P
                        parts = [pn[:, i, c0:c0 + P] for i in range(TILES)]
                    for i, part in enumerate(parts):
                        mm = pe.transpose(ps[:, 3 + j % JOB_BANKS, i * P:(i + 1) * P], part, ident)
                    mm.then_inc(job_ready.sem, 1)
                pe.wait_ge(job_act.sem, job_act.at(l, job_act.step))
                pe.wait_ge(job_dve.sem, job_dve.at(l, job_dve.step))

            def half(h):
                return slice(64 * (h % 2), 64 * (h % 2) + 64)

            def ret_states(l):
                pe.wait_ge(kx_ready.sem, kx_ready.at(l, 1))
                for i, t in enumerate((1, 2, 0, 0)):
                    for h in range(RET_HEADS):
                        col = (i % 2) * 3 * HD + (h // 2) * HD
                        mm = pe.matmul(ps[half(h), i // 2, col:col + HD], kx[:, i, h * HD:(h + 1) * HD],
                                       pn[:, t, C_RV + h * HD:C_RV + (h + 1) * HD], start=True, stop=True)
                mm.then_inc(state_ready.sem, 1)

            def ret_scores(l, t):
                b = 2 if t != 1 else 0
                if t == 1:
                    pe.wait_ge(state_done.sem, state_done.at(l, 1))
                if t == 2:
                    pe.wait_ge(sc_ready.sem, sc_ready.at(l, 1))
                for h in range(RET_HEADS):
                    mm = pe.matmul(ps[:, b + h % 2, (h // 2) * P:(h // 2 + 1) * P],
                                   rkT[half(h), h // 2, t * P:(t + 1) * P],
                                   rqT[half(h), h // 2, t * P:(t + 1) * P], start=True, stop=True)
                mm.then_inc(sct_ready.sem, 1)

            def ret_out(l, t):
                pe.wait_ge(sc_ready.sem, sc_ready.at(l, t + 1))
                if t:
                    pe.wait_ge(ret_done.sem, ret_done.at(l, t))
                for h in range(RET_HEADS):
                    cols = slice(h * HD, (h + 1) * HD)
                    mm = pe.matmul(ps[:, 4, cols], scb[t % 2][:, h, :],
                                   pn[:, t, C_RV + h * HD:C_RV + (h + 1) * HD], start=True, stop=True)
                if t:
                    for a in range(2):
                        state = s0 if (t == 1) == (a == 0) else snew
                        for h in range(RET_HEADS):
                            col = (3 * a + h // 2) * HD
                            mm = pe.matmul(ps[:, 5 + h % 2, col:col + HD], rqT[half(h), h // 2, t * P:(t + 1) * P],
                                           state[half(h), a, h // 2, :], start=True, stop=True)
                mm.then_inc(ret_ready.sem, 1)

            def scores(l, u):
                kind, t, h = ATT[u]
                if u >= 2:
                    pe.wait_ge(exp_done.sem, exp_done.at(l, u - 1))
                elif u == 0:
                    pe.wait_ge(ret_done.sem, ret_done.at(l, 3))
                keys = slice(0, P) if t == 0 else slice(P, 512)
                n = keys_of(t)
                if kind == "na":
                    mm = pe.matmul(ps[:, 2 * (u % 2), 0:n], nqT[half(h), h // 2, t * P:(t + 1) * P],
                                   nkT[half(h), h // 2, keys], start=True, stop=True)
                else:
                    for i in range(2):
                        at32 = 64 * (h % 2) + 32 * i
                        mm = pe.matmul(ps[:, 2 * (u % 2) + i, 0:n],
                                       dqT[at32:at32 + 32, h // 2, t * P:(t + 1) * P],
                                       dkT[at32:at32 + 32, h // 2, keys], start=True, stop=True)
                mm.then_inc(scores_ready.sem, 1)

            def probs_T(l, u):
                kind, t, h = ATT[u]
                if kind == "na":
                    pe.wait_ge(exp_done.sem, exp_done.at(l, u + 1))
                else:
                    pe.wait_ge(diffs_ready.sem, diffs_ready.at(l, u + 1))
                if u >= 2:
                    pe.wait_ge(probsT_copied.sem, probsT_copied.at(l, u - 1))
                for i in range(keys_of(t) // P):
                    mm = pe.transpose(ps[:, 4 + u % 2, i * P:(i + 1) * P], eb[u % 2][:, 0, i * P:(i + 1) * P], ident)
                mm.then_inc(probsT_ready.sem, 1)

            def values(l, u):
                kind, t, h = ATT[u]
                pe.wait_ge(probsT_copied.sem, probsT_copied.at(l, u + 1))
                if u >= 2:
                    pe.wait_ge(head_done.sem, head_done.at(l, u - 1))
                cols = slice(h * HD, (h + 1) * HD)
                c0 = C_NV if kind == "na" else C_DV
                own = slice(c0 + h * HD, c0 + (h + 1) * HD)
                cache = na_vc if kind == "na" else df_vc
                vs = [pn[:, 0, own]] if t == 0 else [pn[:, 1, own], pn[:, 2, own], cache[:, cols]]
                for i, v in enumerate(vs):
                    mm = pe.matmul(ps[:, 6 + u % 2, 0:HD], pTb[u % 2][:, i, :], v,
                                   start=(i == 0), stop=(i == len(vs) - 1))
                mm.then_inc(head_ready.sem, 1)

            def mix_block(ch, t):
                c0 = C_NAO + ch * P if ch < 3 else C_RETO + (ch - 3) * P if ch < 6 else C_DIFFO + (ch - 6) * P
                return pn[:, t, c0:c0 + P]

            def mix_T(l):
                pe.wait_ge(head_done.sem, head_done.at(l, N_ATT))
                pe.wait_ge(ret_normed.sem, ret_normed.at(l, 1))
                pe.wait_ge(diff_normed.sem, diff_normed.at(l, 1))
                for ch in range(CH):
                    if ch >= 2:
                        done = (mixT_act, mixT_dve)[ch % 2]
                        pe.wait_ge(done.sem, done.at(l, ch // 2))
                    for t in range(TILES):
                        mm = pe.transpose(ps[:, 6 + ch % 2, t * P:(t + 1) * P], mix_block(ch, t), ident)
                    mm.then_inc(mixT_ready.sem, 1)

            def out_proj(l, t0, u):
                n = UNIT_OF["wout", u]
                full_static(pe, l, t0, n)
                if u == 0:
                    pe.wait_ge(mixT_act.sem, mixT_act.at(l, CH // 2))
                    pe.wait_ge(mixT_dve.sem, mixT_dve.at(l, CH // 2))
                for t in range(TILES):
                    for ch in range(CH):
                        mm = pe.matmul(ps[:, 2 * t + u // 2, (u % 2) * UCOL:(u % 2 + 1) * UCOL],
                                       mixT[:, ch, t * P:(t + 1) * P], unit(n)[:, ch, :],
                                       start=(ch == 0), stop=(ch == CH - 1))
                mm.then_inc(y_ready.sem, 1)

            def router(l):
                pe.wait_ge(h2_ready.sem, h2_ready.at(l, TILES))
                pe.wait_ge(bc_copied.sem, bc_copied.at(l, 6))
                for ch in range(CH):
                    if ch >= 2:
                        done = (h2T_act, h2T_dve)[ch % 2]
                        pe.wait_ge(done.sem, done.at(l, ch // 2))
                    for t in range(TILES):
                        mm = pe.transpose(ps[:, 6 + ch % 2, t * P:(t + 1) * P], h2[:, t, ch::CH], ident)
                    mm.then_inc(h2T_ready.sem, 1)
                pe.wait_ge(h2T_act.sem, h2T_act.at(l, CH // 2))
                pe.wait_ge(h2T_dve.sem, h2T_dve.at(l, CH // 2))
                for t in range(TILES):
                    for ch in range(CH):
                        mm = pe.matmul(ps[:, 5, t * 64:t * 64 + GROUPS + EXPERTS], h2T[:, ch, t * P:(t + 1) * P],
                                       rw[:, ch, :], start=(ch == 0), stop=(ch == CH - 1))
                mm.then_inc(logits_ready.sem, 1)
                pe.wait_ge(chosen.sem, chosen.at(l, 1))
                for t in range(TILES + 1):
                    lhs = [ones] * min(t, TILES) + ([kc[:, K_TRI:K_TRI + P]] if t < TILES else [])
                    for i, m in enumerate(lhs):
                        mm = pe.matmul(ps[:, 4, t * EXPERTS:(t + 1) * EXPERTS], m, mcount[:, i, :],
                                       start=(i == 0), stop=(i == len(lhs) - 1))
                mm.then_inc(ranks_ready.sem, 1)

            def trip(l, t, g):
                pe.wait_ge(gsel_ready.sem, gsel_ready.at(t, 1))
                pe.wait_ge(hid_ready.sem, hid_ready.at(t, 0))
                pe.wait_ge(idx_known.sem, idx_known.at(t, 0))
                for ch in range(CH):
                    if ch >= 4:
                        done = (xg_act, xg_dve)[ch % 2]
                        pe.wait_ge(done.sem, done.at(t, (ch - 4) // 2 + 1))
                    for i in range(TILES):
                        mm = pe.matmul(ps[:, ch % 4, :], h2[:, i, ch::CH],
                                       gsel[:, i, :, :].rearrange("p e s -> p (e s)"),
                                       start=(i == 0), stop=(i == TILES - 1))
                    mm.then_inc(xg_ready.sem, 1)
                for i in range(PAIRS):
                    for j in range(TILES):
                        mm = pe.matmul(ps[:, 7, 2 * i:2 * i + 2],
                                       gsel[:, j, 2 * i:2 * i + 2, :].rearrange("p e s -> p (e s)"),
                                       rowid[:, j, bass.ds(g * PER_GROUP + 2 * i, 2)],
                                       start=(j == 0), stop=(j == TILES - 1))
                mm.then_inc(idx_ready.sem, 1)
                pe.wait_ge(xg_act.sem, xg_act.at(t, CH // 2))
                pe.wait_ge(xg_dve.sem, xg_dve.at(t, CH // 2))

                def first_half(i):
                    if i >= 2:
                        pe.wait_ge(hid_ready.sem, hid_ready.at(t, i - 1))
                    for kind, done in ((0, gate_ready), (1, up_ready)):
                        for w in range(2):
                            full_trip(pe, l, t, 6 * i + 2 * kind + w)
                        for ch in range(CH):
                            for w in range(2):
                                e = 2 * i + w
                                slot = (6 * i + 2 * kind + w) % RING
                                mm = pe.matmul(ps[64 * w:64 * w + 64, 2 * (i % 2) + kind, 0:FF],
                                               xg[:, ch, e * SLOTS:(e + 1) * SLOTS],
                                               ring[:, slot, ch * FF:(ch + 1) * FF],
                                               start=(ch == 0), stop=(ch == CH - 1))
                        mm.then_inc(done.sem, 1)

                def second_half(i):
                    pe.wait_ge(hid_ready.sem, hid_ready.at(t, i + 1))
                    pe.wait_ge(hidT_copied.sem, hidT_copied.at(t, i))
                    for j in range(2):
                        mm = pe.transpose(ps[:, 4, j * P:(j + 1) * P], hid[i % 2][:, j::2], ident)
                    mm.then_inc(hidT_ready.sem, 1)

                def down(i):
                    pe.wait_ge(hidT_copied.sem, hidT_copied.at(t, i + 1))
                    pe.wait_ge(row_act.sem, row_act.at(t, i))
                    pe.wait_ge(row_dve.sem, row_dve.at(t, i))
                    for w in range(2):
                        full_trip(pe, l, t, 6 * i + 4 + w)
                    for n in range(2):
                        for j in range(2):
                            for w in range(2):
                                slot = (6 * i + 4 + w) % RING
                                mm = pe.matmul(ps[64 * w:64 * w + 64, 5 + n, :],
                                               hidT[i % 2][:, j, 64 * w:64 * w + 64],
                                               ring[:, slot, j * D + n * 512:j * D + (n + 1) * 512],
                                               start=(j == 0), stop=(j == 1))
                    mm.then_inc(down_ready.sem, 1)

                for i in range(PAIRS):
                    first_half(i)
                    if i:
                        down(i - 1)
                    second_half(i)
                down(PAIRS - 1)

            with pe.Fori(0, DEPTH) as l:
                t0 = trips_before(pe, l)
                pe.wait_ge(row_act.sem, row_act.at(t0, 0))
                pe.wait_ge(row_dve.sem, row_dve.at(t0, 0))
                pe.wait_ge(bc_copied.sem, bc_copied.at(l, 0))
                for kind, i in ORDER:
                    if kind == "mod":
                        mod_unit(l, t0, i)
                    elif kind == "col":
                        mod_cols(l, i)
                    elif kind == "xT":
                        pe.wait_ge(x_in.sem, 32)
                        pe.wait_ge(ln2_done.sem, ln2_done.at(l, 0))
                        tokens_T(l)
                    else:
                        project(l, t0, i)
                turns(l)
                ret_states(l)
                pe.wait_ge(modc_ready.sem, modc_ready.at(l, 6))
                for t in range(TILES):
                    ret_scores(l, t)
                    if t:
                        ret_out(l, t - 1)
                ret_out(l, TILES - 1)
                for u in range(N_ATT + 2):
                    if u < N_ATT:
                        scores(l, u)
                    if 1 <= u <= N_ATT:
                        probs_T(l, u - 1)
                    if u >= 2:
                        values(l, u - 2)
                mix_T(l)
                for u in range(OUT_UNITS):
                    out_proj(l, t0, u)
                for n, (s, k) in enumerate(((2, 0), (2, 1), (4, 0), (3, 0), (4, 1), (3, 1))):
                    broadcast(l, n, s, k)
                router(l)
                r1 = rounds_after(pe, l)
                r0 = rounds_before(pe, l)
                with pe.Fori(r0, r1) as r:
                    with pe.Fori(0, GROUPS) as g:
                        t, after = trips_of(pe, l, r0, r, g)
                        with pe.If(after > t):
                            trip(l, t, g)
                t1 = trips_before(pe, l + 1)
                pe.wait_ge(row_act.sem, row_act.at(t1, 0))
                pe.wait_ge(row_dve.sem, row_dve.at(t1, 0))
                pe.wait_ge(idx_known.sem, idx_known.at(t1, 0))
                for n, k in ((6, 0), (7, 1)):
                    broadcast(l, n, 5, k)

        def drain_to(kind, what, where):
            if kind == "pT":
                dst = nqT[:, what, :] if what < 3 else nkT[:, what - 3, 0:TOKENS] if what < 6 else rqT[:, what - 9, :]
                return TOKENS, dst
            if kind == "pN":
                c0 = col_of_block(what[0])
                return len(what) * P, pn[:, where[1], c0:c0 + len(what) * P]
            if kind == "nkc":
                return NA_W, nkc
            if kind == "ck":
                return NA_W, nkT[:, :, TOKENS:512]
            if kind == "cdk":
                return DIFF_W, dkT[:, :, TOKENS:512]
            return TOKENS, {"rkT": rkT, "dqT": dqT, "dkT": dkT}[kind][:, what, 0:TOKENS]

        def job_view(j, n, dst):
            src = ps[:, 3 + j % JOB_BANKS, 0:n]
            return src.rearrange("p (a b) -> p a b", b=P) if len(dst.shape) == 3 else src

        @block.scalar
        def _(act):
            n_rows, n_cols = 2 * WIN_ROWS - 1, 2 * WIN_COLS - 1
            for l in range(DEPTH):
                for b in range(2):
                    for h in range(NA_HEADS):
                        off = ((l * NA_HEADS + h) * n_rows + 5 - b) * n_cols + WIN_COLS - 1
                        act.dma_start(toeplitz[l, b].rearrange("p (h r c) -> h r p c", h=NA_HEADS, r=6)[h],
                                      bass.AP(na_rel_bias.tensor, off, [[n_cols, 6], [-1, GRID_W], [1, GRID_W]]))\
                            .then_inc(toeplitz_out.sem, 16)
            act.wait_ge(const_in.sem, 48)
            act.wait_ge(cond_zero.sem, 3)
            act.activation(cond[:, :, 0:2], condraw[:, :, :].rearrange("p k c -> p c k"), ACT.Silu)\
                .then_inc(cond_ready.sem, 1)

            def tables(l):
                act.wait_ge(lg_a.sem, lg_a.at(l, 1))
                act.activation(lg[:, 1], lg[:, 0], ACT.Exp, scale=-1.0).then_inc(lg_b.sem, 1)
                act.wait_ge(lg_b.sem, lg_b.at(l, 1))
                act.activation(lg[:, 2], lg[:, 1], ACT.Ln, bias=ones[:, 0:1]).then_inc(lg_b.sem, 1)
                act.wait_ge(lg_c.sem, lg_c.at(l, 1))
                for a, (qc, kcol) in enumerate(((K_IP1, K_127J), (K_128I, K_J))):
                    act.activation(qdec[:, a, :], lg[:, 3, a, :], ACT.Exp, scale=kc[:, qc:qc + 1])\
                        .then_inc(tables_ready.sem, 1)
                    act.activation(kdec[:, a, :], lg[:, 3, a, :], ACT.Exp, scale=kc[:, kcol:kcol + 1])\
                        .then_inc(tables_ready.sem, 1)
                    for b in range(2):
                        hp = slice(64 * b, 64 * b + 64)
                        act.activation(cdec[hp, a, :], lg[hp, 3, a, b::2], ACT.Exp, scale=float(P))\
                            .then_inc(tables_ready.sem, 1)
                act.wait_ge(dec_exponent.sem, dec_exponent.at(l, 1))
                act.activation(decay[:, :, :], decay[:, :, :], ACT.Exp).then_inc(tables_ready.sem, 1)
                act.wait_ge(lam_dot.sem, lam_dot.at(l, 1))
                act.activation(lam[:, 2:4], lam[:, 0:2], ACT.Exp).then_inc(lam_exp.sem, 1)

            def drain_job(l, j):
                if DRAIN[j] != "act":
                    return
                kind, what, where = JOBS[j]
                act.wait_ge(job_ready.sem, job_ready.at(l, j + 1))
                if kind == "xT":
                    for k, cols in enumerate((slice(0, P), slice(P, TOKENS))):
                        ins = act.activation(hT[:, what, cols], ps[:, 3 + j % JOB_BANKS, cols], ACT.Identity,
                                             bias=modc[:, 0, what, k:k + 1], scale=modc[:, 1, what, k:k + 1])
                    ins.then_inc(job_act.sem, 1)
                    return
                n, dst = drain_to(kind, what, where)
                act.activation(dst, job_view(j, n, dst), ACT.Copy, scale=RET_SCALE if kind == "rkT" else 1.0)\
                    .then_inc(job_act.sem, 1)

            def exponentials(l, u):
                kind, t, h = ATT[u]
                n = keys_of(t)
                act.wait_ge(negmax_ready.sem, negmax_ready.at(l, u + 1))
                if u >= 2:
                    act.wait_ge(probsT_ready.sem, probsT_ready.at(l, u - 1))
                if kind == "na" and t:
                    act.activation(eb[u % 2][:, 0, 0:n], eb[u % 2][:, 0, 0:n], ACT.Exp, bias=stats[:, u, 0:1],
                                   accum_out=stats[:, u, 2:3]).then_inc(exp_done.sem, 1)
                elif kind == "na":
                    act.activation(eb[u % 2][:, 0, 0:n], ps[:, 2 * (u % 2), 0:n], ACT.Exp, bias=stats[:, u, 0:1],
                                   scale=NA_SCALE, accum_out=stats[:, u, 2:3]).then_inc(exp_done.sem, 1)
                else:
                    for i in range(2):
                        ins = act.activation(eb[u % 2][:, i, 0:n], ps[:, 2 * (u % 2) + i, 0:n], ACT.Exp,
                                             bias=stats[:, u, i:i + 1], scale=DIFF_SCALE,
                                             accum_out=stats[:, u, 2 + i:3 + i])
                    ins.then_inc(exp_done.sem, 1)

            def copy_probs_T(l, u):
                n = keys_of(ATT[u][1])
                act.wait_ge(probsT_ready.sem, probsT_ready.at(l, u + 1))
                if u >= 2:
                    act.wait_ge(head_ready.sem, head_ready.at(l, u - 1))
                act.activation(pTb[u % 2].rearrange("p a b -> p (a b)")[:, 0:n], ps[:, 4 + u % 2, 0:n], ACT.Copy)\
                    .then_inc(probsT_copied.sem, 1)

            def copy_broadcast(l, n, dst):
                act.wait_ge(bc_ready.sem, bc_ready.at(l, n + 1))
                act.activation(dst.rearrange("p (n c) -> p c n", c=CH),
                               ps[:, 6:8, :].rearrange("p b (c n) -> p (b c) n", n=P), ACT.Copy)\
                    .then_inc(bc_copied.sem, 1)

            def trip(l, t):
                for ch in range(0, CH, 2):
                    act.wait_ge(xg_ready.sem, xg_ready.at(t, ch + 1))
                    act.activation(xg[:, ch, :], ps[:, ch % 4, :], ACT.Copy).then_inc(xg_act.sem, 1)

                def silu(i):
                    act.wait_ge(gate_ready.sem, gate_ready.at(t, i + 1))
                    act.activation(sil[i % 2], ps[:, 2 * (i % 2), 0:FF], ACT.Silu).then_inc(silu_done.sem, 1)

                def turn(i):
                    act.wait_ge(hidT_ready.sem, hidT_ready.at(t, i + 1))
                    act.activation(hidT[i % 2].rearrange("p a b -> p (a b)"), ps[:, 4, 0:2 * P], ACT.Copy)\
                        .then_inc(hidT_copied.sem, 1)

                def rows_half(i):
                    act.wait_ge(down_ready.sem, down_ready.at(t, i + 1))
                    act.wait_ge(rows_stored.sem, rows_stored.at(t, i - 1))
                    act.activation(yb[i % 2][:, 0:512], ps[:, 5, :], ACT.Copy).then_inc(row_act.sem, 1)

                for i in range(PAIRS):
                    silu(i)
                    if i:
                        rows_half(i - 1)
                    turn(i)
                rows_half(PAIRS - 1)
            with act.Fori(0, DEPTH) as l:
                act.wait_ge(modc_ready.sem, modc_ready.at(l, 2))
                for kind, i in ORDER:
                    if kind == "xT":
                        for j in range(CH):
                            drain_job(l, j)
                        tables(l)
                    elif kind == "win":
                        for j, job in enumerate(JOBS[CH:FIRST_EXTRA], CH):
                            if (job[2] if job[0] == "pT" else job[2][0]) == i:
                                drain_job(l, j)
                for t in range(TILES):
                    if t == 0:
                        act.wait_ge(job_act.sem, job_act.at(l, DRAINED["act"][FIRST_EXTRA - 1]))
                        act.wait_ge(job_dve.sem, job_dve.at(l, DRAINED["dve"][FIRST_EXTRA - 1]))
                    act.activation(pn[:, t, C_RG:C_RG + RET_W], pn[:, t, C_RG:C_RG + RET_W], ACT.Silu)\
                        .then_inc(swish_ready.sem, 1)
                for j in range(FIRST_EXTRA, len(JOBS)):
                    drain_job(l, j)
                for u in range(N_ATT + 1):
                    if u == 0:
                        act.wait_ge(ret_done.sem, ret_done.at(l, 3))
                    if u < N_ATT:
                        exponentials(l, u)
                    if u >= 1:
                        copy_probs_T(l, u - 1)
                act.wait_ge(head_done.sem, head_done.at(l, N_ATT))
                act.wait_ge(ret_normed.sem, ret_normed.at(l, 1))
                act.wait_ge(diff_normed.sem, diff_normed.at(l, 1))
                one = bass.ds(l, 1)
                act.dma_start(lnw, ln1_w[one].to_broadcast([P, D])).then_inc(ln1_in.sem, 16)
                act.dma_start(lnb, ln1_b[one].to_broadcast([P, D])).then_inc(ln1_in.sem, 16)
                for ch in range(0, CH, 2):
                    act.wait_ge(mixT_ready.sem, mixT_ready.at(l, ch + 1))
                    act.activation(mixT[:, ch, :], ps[:, 6, 0:TOKENS], ACT.Copy).then_inc(mixT_act.sem, 1)
                act.wait_ge(results_out.sem, results_out.at(l, results_out.step))
                copy_broadcast(l, 0, gate)
                act.wait_ge(gated.sem, gated.at(l, 1))
                copy_broadcast(l, 1, gate)
                copy_broadcast(l, 2, s2)
                copy_broadcast(l, 3, t2)
                act.wait_ge(h2_ready.sem, h2_ready.at(l, 1))
                copy_broadcast(l, 4, s2)
                copy_broadcast(l, 5, t2)
                for ch in range(0, CH, 2):
                    act.wait_ge(h2T_ready.sem, h2T_ready.at(l, ch + 1))
                    act.activation(h2T[:, ch, :], ps[:, 6, 0:TOKENS], ACT.Copy).then_inc(h2T_act.sem, 1)
                act.wait_ge(gexp_in.sem, gexp_in.at(l, 1))
                act.activation(gtmp, gtmp, ACT.Exp).then_inc(gexp_done.sem, 1)
                act.wait_ge(gexp_in.sem, gexp_in.at(l, 2))
                act.activation(gst[:, 4, :], gst[:, 4, :], ACT.Exp).then_inc(gexp_done.sem, 1)
                rounds_after(act, l)
                t1 = trips_before(act, l + 1)
                with act.Fori(trips_before(act, l), t1) as t:
                    trip(l, t)
                act.wait_ge(down_ready.sem, down_ready.at(t1, 0))
                act.dma_start(lnw, ln2_w[one].to_broadcast([P, D])).then_inc(ln2_in.sem, 16)
                act.dma_start(lnb, ln2_b[one].to_broadcast([P, D])).then_inc(ln2_in.sem, 16)
                act.wait_ge(rows_stored.sem, rows_stored.at(t1, 0))
                for t in range(TILES):
                    act.dma_start(gath[:, t, :, :].rearrange("p k d -> p (k d)"),
                                  rows[1 + 2 * t * P:1 + 2 * (t + 1) * P].rearrange("(p k) d -> p (k d)", k=2))\
                        .then_inc(gathered[t].sem, 16)
                copy_broadcast(l, 6, gate)
                act.wait_ge(combined.sem, combined.at(l, 1))
                copy_broadcast(l, 7, gate)

        @block.vector
        def _(dve):
            dve.memset(cond[:, :, :], 0.0).then_inc(cond_zero.sem, 1)
            dve.memset(rounds[:, :], 0.0).then_inc(cond_zero.sem, 1)
            dve.memset(trips[:, :], 0.0).then_inc(cond_zero.sem, 1)
            dve.wait_ge(cond_zero.sem, 3)
            dve.wait_ge(const_in.sem, 48)

            def mod_unit(l, q):
                dve.wait_ge(mod_ready.sem, mod_ready.at(l, q + 1))
                if q % 4 == 0 and q:
                    dve.wait_ge(col_ready.sem, col_ready.at(l, q // 4))
                cols = slice((q % 4) * UCOL, (q % 4 + 1) * UCOL)
                dve.tensor_copy(modrow[:, cols], ps[:, q % 2, 0:UCOL]).then_inc(mod_copied.sem, 1)

            def mod_cols(l, s, chain):
                dve.wait_ge(col_ready.sem, col_ready.at(l, s + 1))
                src = ps[:, 2, s * 2 * CH:(s + 1) * 2 * CH].rearrange("p (c k) -> p c k", k=2)
                add = dve.tensor_tensor(modc[:, s, :, :], src, bmod[:, s, :].unsqueeze(2).to_broadcast([P, CH, 2]),
                                        ALU.add)
                if s in (1, 4):
                    chain.link(add)
                    add = dve.tensor_scalar(modc[:, s, :, :], modc[:, s, :, :], 1.0, None, ALU.add)
                add.then_inc(modc_ready.sem, 1)

            def drain_job(l, j):
                if DRAIN[j] != "dve":
                    return
                kind, what, where = JOBS[j]
                dve.wait_ge(job_ready.sem, job_ready.at(l, j + 1))
                if kind == "xT":
                    for k, cols in enumerate((slice(0, P), slice(P, TOKENS))):
                        ins = dve.tensor_scalar(hT[:, what, cols], ps[:, 3 + j % JOB_BANKS, cols],
                                                modc[:, 1, what, k:k + 1], modc[:, 0, what, k:k + 1],
                                                ALU.mult, ALU.add)
                    ins.then_inc(job_dve.sem, 1)
                    return
                n, dst = drain_to(kind, what, where)
                if kind == "rkT":
                    dve.tensor_scalar(dst, job_view(j, n, dst), RET_SCALE, None, ALU.mult).then_inc(job_dve.sem, 1)
                else:
                    dve.tensor_copy(dst, job_view(j, n, dst)).then_inc(job_dve.sem, 1)

            def tables(l, chain):
                chain.link(dve.tensor_scalar(lg[:, 0], dec[:, :, :], -1.0, None, ALU.mult))
                dve.tensor_tensor(lg[:, 0], lg[:, 0], dec[:, :, :], ALU.max).then_inc(lg_a.sem, 1)
                chain.link(dve.tensor_tensor(lamt[:, :, :], lamp[:, 0::2, :], lamp[:, 1::2, :], ALU.mult))
                dve.tensor_reduce(lam[:, 0:2], lamt[:, :, :], AX.X, ALU.add).then_inc(lam_dot.sem, 1)
                dve.wait_ge(lg_b.sem, lg_b.at(l, 2))
                chain.link(dve.tensor_scalar(lg[:, 3], dec[:, :, :], 0.0, None, ALU.min))
                dve.tensor_tensor(lg[:, 3], lg[:, 3], lg[:, 2], ALU.subtract).then_inc(lg_c.sem, 1)
                dve.wait_ge(lg_c.sem, lg_c.at(l, 1))
                for h in range(RET_HEADS):
                    ins = dve.tensor_scalar(decay[:, h, :], kc[:, K_A:K_A + P], lg[:, 3, 0, h:h + 1], None, ALU.mult)
                chain.link(ins)
                for h in range(RET_HEADS):
                    ins = dve.scalar_tensor_tensor(decay[:, h, :], kc[:, K_B:K_B + P], lg[:, 3, 1, h:h + 1],
                                                   decay[:, h, :], ALU.mult, ALU.add)
                ins.then_inc(dec_exponent.sem, 1)
                dve.wait_ge(tables_ready.sem, tables_ready.at(l, 9))
                dve.tensor_scalar(kdec[:, :, :], kdec[:, :, :], RET_SCALE, None, ALU.mult).then_inc(kdec_scaled.sem, 1)
                dve.wait_ge(lam_exp.sem, lam_exp.at(l, 1))
                chain.link(dve.tensor_tensor(lam[:, 4:5], lam[:, 3:4], lam[:, 2:3], ALU.subtract))
                dve.tensor_tensor(lam[:, 4:5], lam[:, 4:5], lamk[:, 0:1], ALU.subtract).then_inc(lam_ready.sem, 1)

            def rotate(l, chain):
                for t in (1, 2):
                    xs = pn[:, t, C_DQ:C_DQ + 512].rearrange("p (g d) -> p g d", d=DIFF_D)
                    halves = pn[:, t, C_DQ:C_DQ + 512].rearrange("p (g x d) -> p g x d", x=2, d=8)
                    cos = kc[:, K_COS + 32 * (t - 1):K_COS + 32 * t]
                    sin = kc[:, K_SIN + 32 * (t - 1):K_SIN + 32 * t].rearrange("p (a x d) -> p a x d", x=2, d=8)
                    sw = at(ROPE_T, 512)
                    swh = sw.rearrange("p (g x d) -> p g x d", x=2, d=8)
                    for xx in range(2):
                        src = halves[:, :, 1 - xx, :].rearrange("p (g a) d -> p g a d", a=2)
                        dst = swh[:, :, xx, :].rearrange("p (g a) d -> p g a d", a=2)
                        tab = sin[:, :, xx, :].unsqueeze(1).to_broadcast([P, 16, 2, 8])
                        ins = dve.tensor_tensor(dst, src, tab, ALU.mult)
                    chain.link(ins)
                    chain.link(dve.tensor_tensor(xs, xs, cos.unsqueeze(1).to_broadcast([P, 16, DIFF_D]), ALU.mult))
                    ins = dve.tensor_tensor(xs, xs, sw.rearrange("p (g d) -> p g d", d=DIFF_D), ALU.add)
                    if t == 1:
                        chain.link(ins)
                ins.then_inc(rope_done.sem, 1)

            def heads(v):
                return v.rearrange("p (h d) -> p h d", d=HD)

            def over(v, n):
                return v.unsqueeze(2).to_broadcast([P, v.shape[1], n])

            def retention(l, chain):
                dve.wait_ge(job_act.sem, job_act.at(l, job_act.step))
                dve.wait_ge(kdec_scaled.sem, kdec_scaled.at(l, 1))
                for i, (t, a) in enumerate(((1, 0), (2, 1), (0, 0), (0, 1))):
                    ins = dve.tensor_tensor(heads(kx[:, i, :]), heads(pn[:, t, C_RK:C_RK + RET_W]),
                                            over(kdec[:, a, :], HD), ALU.mult)
                ins.then_inc(kx_ready.sem, 1)
                dve.wait_ge(state_ready.sem, state_ready.at(l, 1))
                dve.tensor_copy(sctx.rearrange("p a b c -> p (a b c)"), ps[:, 1, 0:6 * HD])
                s6 = "p a b c -> p (a b) c"
                chain.link(dve.tensor_tensor(snew.rearrange(s6), s0[:, :, :, :].rearrange(s6),
                                             over(cdec[:, :, :].rearrange("p a b -> p (a b)"), HD), ALU.mult))
                dve.tensor_tensor(snew.rearrange("p a b c -> p (a b c)"), snew.rearrange("p a b c -> p (a b c)"),
                                  ps[:, 0, 0:6 * HD], ALU.add).then_inc(state_done.sem, 1)
                dve.wait_ge(state_done.sem, state_done.at(l, 1))

                def decayed(t):
                    b = 2 if t != 1 else 0
                    dve.wait_ge(sct_ready.sem, sct_ready.at(l, t + 1))
                    if t == 2:
                        dve.wait_ge(ret_ready.sem, ret_ready.at(l, 1))
                    for w in range(2):
                        ins = dve.tensor_tensor(scb[t % 2][:, w::2, :],
                                                ps[:, b + w, 0:3 * P].rearrange("p (h i) -> p h i", i=P),
                                                decay[:, w::2, :], ALU.mult)
                    ins.then_inc(sc_ready.sem, 1)

                def add_up(t):
                    out = pn[:, t, C_RETO:C_RETO + RET_W]
                    dve.wait_ge(ret_ready.sem, ret_ready.at(l, t + 1))
                    if t == 0:
                        dve.tensor_copy(out, ps[:, 4, 0:RET_W]).then_inc(ret_done.sem, 1)
                        return
                    for w in range(2):
                        for a in range(2):
                            ins = dve.tensor_tensor(heads(rt[:, a, :])[:, w::2, :],
                                                    heads(ps[:, 5 + w, 3 * a * HD:3 * (a + 1) * HD]),
                                                    over(qdec[:, a, w::2], HD), ALU.mult)
                    chain.link(ins)
                    chain.link(dve.tensor_tensor(rt[:, 0, :], rt[:, 0, :], rt[:, 1, :], ALU.add))
                    dve.tensor_tensor(out, rt[:, 0, :], ps[:, 4, 0:RET_W], ALU.add).then_inc(ret_done.sem, 1)

                decayed(0)
                for t in range(TILES):
                    if t + 1 < TILES:
                        decayed(t + 1)
                    add_up(t)
                dve.wait_ge(ret_done.sem, ret_done.at(l, 3))

            def maxima(l, u, chain):
                kind, t, h = ATT[u]
                n = keys_of(t)
                dve.wait_ge(scores_ready.sem, scores_ready.at(l, u + 1))
                if kind == "na" and t:
                    dve.wait_ge(bias_masked.sem, bias_masked.at(l, 4))
                    dve.wait_ge(probsT_ready.sem, probsT_ready.at(l, u - 1))
                    b0 = 2 - 2 * (t - 1)
                    dve.scalar_tensor_tensor(eb[u % 2][:, 0, 0:LAT], ps[:, 2 * (u % 2), 0:LAT], NA_SCALE,
                                             bias[:, h, b0:b0 + 4, :].rearrange("p a b -> p (a b)"), ALU.mult, ALU.add)
                    chain.link(dve.tensor_scalar(eb[u % 2][:, 0, LAT:n], ps[:, 2 * (u % 2), LAT:n], NA_SCALE, None, ALU.mult))
                    chain.link(dve.tensor_reduce(stats[:, u, 1:2], eb[u % 2][:, 0, 0:n], AX.X, ALU.max))
                    dve.tensor_scalar(stats[:, u, 0:1], stats[:, u, 1:2], -1.0, None, ALU.mult)\
                        .then_inc(negmax_ready.sem, 1)
                elif kind == "na":
                    chain.link(dve.tensor_reduce(stats[:, u, 1:2], ps[:, 2 * (u % 2), 0:n], AX.X, ALU.max))
                    dve.tensor_scalar(stats[:, u, 0:1], stats[:, u, 1:2], -NA_SCALE, None, ALU.mult)\
                        .then_inc(negmax_ready.sem, 1)
                else:
                    b = 2 * (u % 2)
                    chain.link(dve.tensor_reduce(stats[:, u, 4:6], ps[:, b:b + 2, 0:n], AX.X, ALU.max))
                    dve.tensor_scalar(stats[:, u, 0:2], stats[:, u, 4:6], -DIFF_SCALE, None, ALU.mult)\
                        .then_inc(negmax_ready.sem, 1)

            def after_exp(l, u, chain):
                kind, t, h = ATT[u]
                n = keys_of(t)
                dve.wait_ge(exp_done.sem, exp_done.at(l, u + 1))
                if kind == "na":
                    chain.link(dve.reciprocal(stats[:, u, 3:4], stats[:, u, 2:3]))
                    return
                e = eb[u % 2]
                chain.link(dve.reciprocal(stats[:, u, 4:6], stats[:, u, 2:4]))
                if u == 0:
                    dve.wait_ge(lam_ready.sem, lam_ready.at(l, 1))
                dve.tensor_scalar(e[:, 0, 0:n], e[:, 0, 0:n], stats[:, u, 4:5], None, ALU.mult)
                chain.link(dve.tensor_scalar(stats[:, u, 5:6], stats[:, u, 5:6], lam[:, 4:5], None, ALU.mult))
                dve.scalar_tensor_tensor(e[:, 0, 0:n], e[:, 1, 0:n], stats[:, u, 5:6], e[:, 0, 0:n],
                                         ALU.mult, ALU.add).then_inc(diffs_ready.sem, 1)

            def head_out(l, u):
                kind, t, h = ATT[u]
                dve.wait_ge(head_ready.sem, head_ready.at(l, u + 1))
                if kind == "na":
                    if t == 0 and h == 0:
                        dve.wait_ge(results_out.sem, results_out.at(l, results_out.step))
                    dve.tensor_scalar(pn[:, t, C_NAO + h * HD:C_NAO + (h + 1) * HD], ps[:, 6 + u % 2, 0:HD],
                                      stats[:, u, 3:4], None, ALU.mult).then_inc(head_done.sem, 1)
                else:
                    dve.tensor_copy(pn[:, t, C_DIFFO + h * HD:C_DIFFO + (h + 1) * HD], ps[:, 6 + u % 2, 0:HD])\
                        .then_inc(head_done.sem, 1)

            def ret_moments(l, chain):
                r = pn[:, :, C_RETO:C_RETO + RET_W].rearrange("p t (h d) -> p t h d", d=HD)

                def wide(i):
                    return norm_s[:, i, :].rearrange("p (t h) -> p t h", t=TILES).unsqueeze(3)\
                        .to_broadcast([P, TILES, RET_HEADS, HD])

                for t in range(TILES):
                    ins = dve.tensor_reduce(norm_s[:, 0, t * RET_HEADS:(t + 1) * RET_HEADS],
                                            r[:, t, :, :], AX.X, ALU.add)
                chain.link(ins)
                chain.link(dve.tensor_scalar(norm_s[:, 1, :], norm_s[:, 0, :], -1.0 / HD, None, ALU.mult))
                chain.link(dve.tensor_tensor(r, r, wide(1), ALU.add))
                for t in range(TILES):
                    chain.link(dve.tensor_tensor(sq[:, 0:RET_W], pn[:, t, C_RETO:C_RETO + RET_W],
                                                 pn[:, t, C_RETO:C_RETO + RET_W], ALU.mult))
                    chain.link(dve.tensor_reduce(norm_s[:, 0, t * RET_HEADS:(t + 1) * RET_HEADS],
                                                 heads(sq[:, 0:RET_W]), AX.X, ALU.add))
                dve.tensor_scalar(norm_s[:, 2, :], norm_s[:, 0, :], 1.0 / HD, LN_EPS, ALU.mult, ALU.add)\
                    .then_inc(ret_var.sem, 1)

            def diff_moments(l, chain):
                for t in range(TILES):
                    o = pn[:, t, C_DIFFO:C_DIFFO + DIFF_W]
                    chain.link(dve.tensor_tensor(sq[:, 0:DIFF_W], o, o, ALU.mult))
                    chain.link(dve.tensor_reduce(diff_s[:, 0, t * DIFF_HEADS:(t + 1) * DIFF_HEADS],
                                                 heads(sq[:, 0:DIFF_W]), AX.X, ALU.add))
                dve.tensor_scalar(diff_s[:, 1, :], diff_s[:, 0, :], 1.0 / HD, LN_EPS, ALU.mult, ALU.add)\
                    .then_inc(diff_var.sem, 1)

            def moments(t, chain, var):
                for i in range(2):
                    ins = dve.bn_stats(ln_s[:, t, 6 * i:6 * i + 6], x[:, t, 512 * i:512 * i + 512])
                chain.link(ins, wait_alone)
                chain.link(dve.bn_aggr(ln_s[:, t, 12:14], ln_s[:, t, 0:12]))
                dve.tensor_scalar(ln_s[:, t, 14:15], ln_s[:, t, 13:14], LN_EPS, None, ALU.add).then_inc(var.sem, 1)

            def normalise(l, t, chain, rstd, arrived, done):
                dve.wait_ge(rstd.sem, rstd.at(l, t + 1))
                if t == 0:
                    dve.wait_ge(arrived.sem, arrived.at(l, arrived.step))
                chain.link(dve.tensor_scalar(x[:, t, :], x[:, t, :], ln_s[:, t, 12:13], ln_s[:, t, 15:16],
                                             ALU.subtract, ALU.mult))
                chain.link(dve.tensor_tensor(x[:, t, :], x[:, t, :], lnw, ALU.mult))
                dve.tensor_tensor(x[:, t, :], x[:, t, :], lnb, ALU.add).then_inc(done.sem, 1)
                dve.wait_ge(done.sem, done.at(l, t + 1))

            def pick(src, weights, best, out, tmp, chain, groups_of):
                w = kc[:, weights:weights + groups_of].unsqueeze(1).to_broadcast([P, TILES, groups_of])
                chain.link(dve.tensor_reduce(gst[:, best, :], src, AX.X, ALU.max))
                chain.link(dve.tensor_tensor(tmp, src, over(gst[:, best, :], groups_of), ALU.is_equal))
                chain.link(dve.tensor_tensor(tmp, tmp, w, ALU.mult))
                chain.link(dve.tensor_reduce(gst[:, 7, :], tmp, AX.X, ALU.max))
                chain.link(dve.tensor_tensor(out, tmp, over(gst[:, 7, :], groups_of), ALU.is_equal))

            def choose(l, chain):
                dve.wait_ge(logits_ready.sem, logits_ready.at(l, 1))
                chain.link(dve.tensor_copy(logit, ps[:, 5, 0:TILES * 64].rearrange("p (t e) -> p t e", t=TILES)
                                           [:, :, 0:GROUPS + EXPERTS]))
                pick(logit[:, :, 0:GROUPS], K_TB4, 0, goh, gtmp, chain, GROUPS)
                dve.tensor_tensor(gtmp, logit[:, :, 0:GROUPS], over(gst[:, 0, :], GROUPS), ALU.subtract)\
                    .then_inc(gexp_in.sem, 1)
                chain.link(dve.tensor_scalar(goh, goh, -1.0, -NEG_INF, ALU.add, ALU.mult))
                chain.link(dve.tensor_tensor(em.rearrange("p t (g e) -> p t g e", g=GROUPS),
                                             logit[:, :, GROUPS:].rearrange("p t (g e) -> p t g e", g=GROUPS),
                                             goh.unsqueeze(3).to_broadcast([P, TILES, GROUPS, PER_GROUP]), ALU.add))
                pick(em, K_TB32, 1, oh[:, 0], et, chain, EXPERTS)
                chain.link(dve.scalar_tensor_tensor(em, oh[:, 0], 2 * NEG_INF, em, ALU.mult, ALU.add))
                pick(em, K_TB32, 2, oh[:, 1], et, chain, EXPERTS)
                dve.tensor_tensor(mcount, oh[:, 0], oh[:, 1], ALU.add).then_inc(chosen.sem, 1)
                dve.wait_ge(gexp_done.sem, gexp_done.at(l, 1))
                dve.tensor_tensor(gst[:, 4, :], gst[:, 2, :], gst[:, 1, :], ALU.subtract).then_inc(gexp_in.sem, 1)
                chain.link(dve.tensor_reduce(gst[:, 3, :], gtmp, AX.X, ALU.add))
                dve.wait_ge(gexp_done.sem, gexp_done.at(l, 2))
                chain.link(dve.tensor_scalar(gst[:, 5, :], gst[:, 4, :], 1.0, None, ALU.add))
                chain.link(dve.tensor_tensor(gst[:, 5, :], gst[:, 5, :], gst[:, 3, :], ALU.mult))
                chain.link(dve.reciprocal(wts[:, 0, :], gst[:, 5, :]))
                chain.link(dve.tensor_tensor(wts[:, 1, :], wts[:, 0, :], gst[:, 4, :], ALU.mult))

            def places(l, chain):
                dve.wait_ge(ranks_ready.sem, ranks_ready.at(l, 1))
                ranks = ps[:, 4, 0:TILES * EXPERTS].rearrange("p (t e) -> p t e", t=TILES)
                chain.link(dve.tensor_scalar(rankm, mcount, -2.0 * TOKENS, 2.0 * TOKENS, ALU.mult, ALU.add))
                chain.link(dve.tensor_tensor(rankm, rankm, ranks, ALU.add))
                for t in range(TILES):
                    ins = dve.scalar_tensor_tensor(rowid[:, t, :], mcount[:, t, :], kc[:, K_ROW + t:K_ROW + t + 1],
                                                   oh[:, 1, t, :], ALU.mult, ALU.add)
                chain.link(ins)
                thr = kc[:, K_THR:K_THR + ROUNDS_MAX]
                most, passed_thr, n_rounds = cmpn[:, 0:GROUPS], cmpn[:, GROUPS:GROUPS + ROUNDS_MAX], cmpn[:, GROUPS + ROUNDS_MAX:GROUPS + ROUNDS_MAX + 1]
                total = ps[:, 4, TILES * EXPERTS:(TILES + 1) * EXPERTS]
                chain.link(dve.tensor_reduce(most, total.rearrange("p (g e) -> p g e", g=GROUPS), AX.X, ALU.max))
                chain.link(dve.tensor_tensor(counts, most.unsqueeze(1).to_broadcast([P, ROUNDS_MAX, GROUPS]),
                                             over(thr, GROUPS), ALU.is_gt))
                chain.link(dve.tensor_reduce(passed_thr, counts, AX.X, ALU.max))
                chain.link(dve.tensor_reduce(n_rounds, passed_thr, AX.X, ALU.add))
                chain.link(dve.tensor_tensor(rounds[0:1, bass.ds(l + 1, 1)], n_rounds[0:1, :],
                                             rounds[0:1, bass.ds(l, 1)], ALU.add))
                for g in range(1, GROUPS):
                    chain.link(dve.tensor_tensor(counts[:, :, g:g + 1], counts[:, :, g:g + 1],
                                                 counts[:, :, g - 1:g], ALU.add))
                for r in range(1, ROUNDS_MAX):
                    chain.link(dve.tensor_tensor(counts[:, r, :], counts[:, r, :],
                                                 counts[:, r - 1, GROUPS - 1:].to_broadcast([P, GROUPS]), ALU.add))
                dve.tensor_tensor(trips[0:1, bass.ds(l * TRIPS_MAX + 1, TRIPS_MAX)],
                                  counts[0:1].rearrange("p r g -> p (r g)"),
                                  trips[0:1, bass.ds(l * TRIPS_MAX, 1)].to_broadcast([1, TRIPS_MAX]), ALU.add)\
                    .then_inc(rounds_known.sem, 1)
                chain.link(dve.tensor_copy(iotar, kc[:, K_IOTA:K_IOTA + SLOTS]))

            def trip(l, t, g):
                dve.wait_ge(xg_ready.sem, xg_ready.at(t, 0))
                for i in range(TILES):
                    cols = rankm[:, i, bass.ds(g * PER_GROUP, PER_GROUP)]
                    ins = dve.tensor_tensor(gsel[:, i, :, :], over(cols, SLOTS),
                                            iotar.unsqueeze(1).to_broadcast([P, PER_GROUP, SLOTS]), ALU.is_equal)
                ins.then_inc(gsel_ready.sem, 1)
                for ch in range(1, CH, 2):
                    dve.wait_ge(xg_ready.sem, xg_ready.at(t, ch + 1))
                    dve.tensor_copy(xg[:, ch, :], ps[:, ch % 4, :]).then_inc(xg_dve.sem, 1)
                dve.wait_ge(rows_stored.sem, rows_stored.at(t, 0))
                dve.wait_ge(idx_ready.sem, idx_ready.at(t, 1))
                for w in range(2):
                    hp = slice(64 * w, 64 * w + 64)
                    ins = dve.tensor_scalar(idxf[hp, :], ps[hp, 7, w:2 * PAIRS:2], 0.5, kc[hp, K_EMPTY:K_EMPTY + 1],
                                            ALU.is_lt, ALU.mult)
                ins.then_inc(idx_link.sem, 1)
                dve.wait_ge(idx_link.sem, idx_link.at(t, 1))
                for w in range(2):
                    hp = slice(64 * w, 64 * w + 64)
                    ins = dve.tensor_tensor(idxu[hp, :], idxf[hp, :], ps[hp, 7, w:2 * PAIRS:2], ALU.add)
                ins.then_inc(idx_known.sem, 1)

                def rows_half(i):
                    dve.wait_ge(down_ready.sem, down_ready.at(t, i + 1))
                    dve.wait_ge(rows_stored.sem, rows_stored.at(t, i - 1))
                    dve.tensor_copy(yb[i % 2][:, 512:D], ps[:, 6, :]).then_inc(row_dve.sem, 1)

                for i in range(PAIRS):
                    dve.wait_ge(silu_done.sem, silu_done.at(t, i + 1))
                    dve.wait_ge(up_ready.sem, up_ready.at(t, i + 1))
                    if i >= 2:
                        dve.wait_ge(hidT_ready.sem, hidT_ready.at(t, i - 1))
                    dve.tensor_tensor(hid[i % 2], sil[i % 2], ps[:, 2 * (i % 2) + 1, 0:FF], ALU.mult)\
                        .then_inc(hid_ready.sem, 1)
                    if i:
                        rows_half(i - 1)
                rows_half(PAIRS - 1)

            with dve.Fori(0, DEPTH) as l:
                chain = Chain(dve, dve_link, l)
                dve.wait_ge(small_in.sem, small_in.at(l, small_in.step))
                for kind, i in ORDER:
                    if kind == "mod":
                        mod_unit(l, i)
                    elif kind == "col":
                        mod_cols(l, i, chain)
                    elif kind == "xT":
                        dve.wait_ge(modc_ready.sem, modc_ready.at(l, 2))
                        for j in range(CH):
                            drain_job(l, j)
                        tables(l, chain)
                    else:
                        for j, job in enumerate(JOBS[CH:FIRST_EXTRA], CH):
                            if (job[2] if job[0] == "pT" else job[2][0]) == i:
                                drain_job(l, j)
                        if i == 12:
                            dve.wait_ge(job_act.sem, job_act.at(l, DRAINED["act"][LAST_JOB[12]]))
                            dve.wait_ge(job_dve.sem, job_dve.at(l, DRAINED["dve"][LAST_JOB[12]]))
                            rotate(l, chain)
                for j in range(FIRST_EXTRA, len(JOBS)):
                    drain_job(l, j)
                retention(l, chain)
                for u in range(N_ATT + 2):
                    if u < N_ATT:
                        maxima(l, u, chain)
                    if 1 <= u <= N_ATT:
                        after_exp(l, u - 1, chain)
                    if u >= 2:
                        head_out(l, u - 2)
                    if u == RET_NORM_AT:
                        ret_moments(l, chain)
                    if u == DIFF_NORM_AT:
                        dve.wait_ge(head_done.sem, head_done.at(l, N_DIFF))
                        diff_moments(l, chain)
                for ch in range(1, CH, 2):
                    dve.wait_ge(mixT_ready.sem, mixT_ready.at(l, ch + 1))
                    dve.tensor_copy(mixT[:, ch, :], ps[:, 7, 0:TOKENS]).then_inc(mixT_dve.sem, 1)
                dve.wait_ge(y_ready.sem, y_ready.at(l, OUT_UNITS))
                for t in range(TILES):
                    dve.wait_ge(bc_copied.sem, bc_copied.at(l, min(t, 1) + 1))
                    dve.tensor_tensor(z.rearrange("p (a b) -> p a b", a=2), ps[:, 2 * t:2 * t + 2, :],
                                      gate.rearrange("p (a b) -> p a b", a=2), ALU.mult).then_inc(gated.sem, 1)
                    dve.wait_ge(gated.sem, gated.at(l, t + 1))
                    chain.link(dve.scalar_tensor_tensor(x[:, t, :], x[:, t, :], ALPHA, z, ALU.mult, ALU.add))
                    moments(t, chain, var1)
                for t in range(TILES):
                    normalise(l, t, chain, rstd1, ln1_in, ln1_done)
                    dve.wait_ge(bc_copied.sem, bc_copied.at(l, 4 if t == 0 else 6))
                    chain.link(dve.tensor_tensor(h2[:, t, :], x[:, t, :], s2, ALU.mult))
                    dve.tensor_tensor(h2[:, t, :], h2[:, t, :], t2, ALU.add).then_inc(h2_ready.sem, 1)
                for ch in range(1, CH, 2):
                    dve.wait_ge(h2T_ready.sem, h2T_ready.at(l, ch + 1))
                    dve.tensor_copy(h2T[:, ch, :], ps[:, 7, 0:TOKENS]).then_inc(h2T_dve.sem, 1)
                choose(l, chain)
                places(l, chain)
                r1 = rounds_after(dve, l)
                r0 = rounds_before(dve, l)
                with dve.Fori(r0, r1) as r:
                    with dve.Fori(0, GROUPS) as g:
                        t, after = trips_of(dve, l, r0, r, g)
                        with dve.If(after > t):
                            trip(l, t, g)
                    dve.tensor_scalar(iotar, iotar, float(SLOTS), None, ALU.add).then_inc(trip_link.sem, 1)
                    dve.wait_ge(trip_link.sem, trip_link.at(r, 1))
                for t in range(TILES):
                    dve.wait_ge(gathered[t].sem, gathered[t].at(l, 16))
                    a, b = gath[:, t, 0, :], gath[:, t, 1, :]
                    chain.link(dve.tensor_scalar(a, a, wts[:, 0, t:t + 1], None, ALU.mult))
                    chain.link(dve.scalar_tensor_tensor(a, b, wts[:, 1, t:t + 1], a, ALU.mult, ALU.add))
                    dve.wait_ge(bc_copied.sem, bc_copied.at(l, 7 if t == 0 else 8))
                    dve.tensor_tensor(a, a, gate, ALU.mult).then_inc(combined.sem, 1)
                    dve.wait_ge(combined.sem, combined.at(l, t + 1))
                    chain.link(dve.scalar_tensor_tensor(x[:, t, :], x[:, t, :], ALPHA, a, ALU.mult, ALU.add))
                    moments(t, chain, var2)
                for t in range(TILES):
                    normalise(l, t, chain, rstd2, ln2_in, ln2_done)
                assert chain.n == DVE_LINKS, chain.n

        @block.gpsimd
        def _(pool):
            pool.wait_ge(const_in.sem, 48)
            pool.wait_ge(cond_zero.sem, 3)

            def mask_bias(l):
                wait_alone(pool, small_in, small_in.at(l, small_in.step))
                rest = GRID_W - WIN_COLS
                for half in range(2):
                    b = bias[64 * half:64 * half + 64, :, :, :].rearrange("p h r c -> p (h r) c")
                    low = b[:, :, 0:rest]
                    pool.affine_select(out=low, in_=low, compare_op=ALU.is_ge, fill=NEG_INF, base=WIN_COLS // 2,
                                       pattern=[[0, 36], [1, rest]], channel_multiplier=-1)\
                        .then_inc(bias_masked.sem, 1)
                    wait_alone(pool, bias_masked, bias_masked.at(l, 2 * half + 1))
                    high = b[:, :, WIN_COLS:]
                    pool.affine_select(out=high, in_=high, compare_op=ALU.is_gt, fill=NEG_INF,
                                       base=WIN_COLS // 2 - WIN_COLS,
                                       pattern=[[0, 36], [-1, rest]], channel_multiplier=1)\
                        .then_inc(bias_masked.sem, 1)
                    wait_alone(pool, bias_masked, bias_masked.at(l, 2 * half + 2))

            def store(dst, src):
                pool.dma_start(dst, src).then_inc(results_out.sem, 16)

            def power(dst, src, n):
                return pool.tensor_tensor(dst, src, kc[:, K_MHALF:K_MHALF + 1].to_broadcast([P, n]), ALU.pow)

            def trip(t):
                pool.wait_ge(idx_known.sem, idx_known.at(t, 1))
                for i in range(PAIRS):
                    pool.wait_ge(row_act.sem, row_act.at(t, i + 1))
                    wait_alone(pool, row_dve, row_dve.at(t, i + 1))
                    pool.indirect_dma_start(rows, bass.IndirectOffsetOnAxis(ap=idxu[:, i:i + 1], axis=0), yb[i % 2],
                                            None, bounds_check=ROWS - 1, oob_is_err=False)\
                        .then_inc(rows_out.sem, 16)
                    pool.wait_ge(rows_out.sem, rows_out.at(t, 16 * (i + 1)))
                    pool.sem_inc(rows_stored.sem, 1)

            with pool.Fori(0, DEPTH) as l:
                chain = Chain(pool, pool_link, l)
                one = bass.ds(l, 1)
                mask_bias(l)
                wait_alone(pool, job_act, job_act.at(l, job_act.step))
                wait_alone(pool, job_dve, job_dve.at(l, job_dve.step))
                store(new_na_k[0, one].rearrange("o p h d -> (o p) (h d)"), nkc)
                store(new_na_v[0, one].rearrange("o p h d -> (o p) (h d)"), pn[:, 0, C_NV:C_NV + NA_W])
                store(new_diff_k[0, one].rearrange("o p h d -> (o p) (h d)"), pn[:, 0, C_DK:C_DK + DIFF_W])
                store(new_diff_v[0, one].rearrange("o p h d -> (o p) (h d)"), pn[:, 0, C_DV:C_DV + DIFF_W])
                wait_alone(pool, state_done, state_done.at(l, 1))
                for b in range(2):
                    store(new_ret_state[0, one, :, b::2].rearrange("o a h k v -> k (o a) h v"),
                          sctx[64 * b:64 * b + 64, :, :, :])
                pool.wait_ge(ret_var.sem, ret_var.at(l, 1))
                chain.link(power(norm_s[:, 3, :], norm_s[:, 2, :], TILES * RET_HEADS))
                pool.wait_ge(swish_ready.sem, swish_ready.at(l, 3))
                for t in range(TILES):
                    r = pn[:, t, C_RETO:C_RETO + RET_W]
                    rh = r.rearrange("p (h d) -> p h d", d=HD)
                    chain.link(pool.tensor_tensor(
                        rh, rh, norm_s[:, 3, t * RET_HEADS:(t + 1) * RET_HEADS].unsqueeze(2)
                        .to_broadcast([P, RET_HEADS, HD]), ALU.mult))
                    chain.link(pool.tensor_tensor(r, r, gnw[:, :], ALU.mult))
                    chain.link(pool.tensor_tensor(r, r, gnb[:, :], ALU.add))
                    ins = pool.tensor_tensor(r, r, pn[:, t, C_RG:C_RG + RET_W], ALU.mult)
                    if t < TILES - 1:
                        chain.link(ins)
                ins.then_inc(ret_normed.sem, 1)
                chain.link(pool.tensor_scalar(dnw[:, :], dnw[:, :], lamk[:, 1:2], 1.0, ALU.mult, ALU.mult))
                pool.wait_ge(diff_var.sem, diff_var.at(l, 1))
                chain.link(power(diff_s[:, 2, :], diff_s[:, 1, :], TILES * DIFF_HEADS))
                for t in range(TILES):
                    o = pn[:, t, C_DIFFO:C_DIFFO + DIFF_W]
                    oh_ = o.rearrange("p (h d) -> p h d", d=HD)
                    chain.link(pool.tensor_tensor(
                        oh_, oh_, diff_s[:, 2, t * DIFF_HEADS:(t + 1) * DIFF_HEADS].unsqueeze(2)
                        .to_broadcast([P, DIFF_HEADS, HD]), ALU.mult))
                    ins = pool.tensor_tensor(o, o, dnw[:, :], ALU.mult)
                    if t < TILES - 1:
                        chain.link(ins)
                ins.then_inc(diff_normed.sem, 1)
                for t in range(TILES):
                    pool.wait_ge(var1.sem, var1.at(l, t + 1))
                    power(ln_s[:, t, 15:16], ln_s[:, t, 14:15], 1).then_inc(rstd1.sem, 1)
                rounds_after(pool, l)
                wait_alone(pool, combined, combined.at(l, 0))
                with pool.Fori(trips_before(pool, l), trips_before(pool, l + 1)) as t:
                    trip(t)
                for t in range(TILES):
                    pool.wait_ge(var2.sem, var2.at(l, t + 1))
                    power(ln_s[:, t, 15:16], ln_s[:, t, 14:15], 1).then_inc(rstd2.sem, 1)
                assert chain.n == POOL_LINKS, chain.n


DVE_LINKS = 196
POOL_LINKS = 19

_INS = ['x_prompt', 'x_sample', 'c', 'cache_na_k', 'cache_na_v', 'state_ret', 'cache_diff_k', 'cache_diff_v', 'c_ctx',
        'w_mod', 'b_mod', 'w_in', 'na_rel_bias', 'ret_decay', 'ret_gn_w', 'ret_gn_b', 'diff_lambda', 'diff_norm_w',
        'w_out', 'ln1_w', 'ln1_b', 'router_group', 'router_expert', 'exp_w_gate', 'exp_w_up', 'exp_w_down',
        'ln2_w', 'ln2_b']
_OUTS = [(1, CTX, D), (1, LAT, D), (1, DEPTH, CTX, NA_HEADS, HD), (1, DEPTH, CTX, NA_HEADS, HD),
         (1, DEPTH, 2, RET_HEADS, HD, HD), (1, DEPTH, CTX, DIFF_HEADS, 2 * DIFF_D), (1, DEPTH, CTX, DIFF_HEADS, HD)]


def kernel(**inputs):
    import concourse.bacc as bacc
    from concourse.bass_utils import run_bass_kernel_spmd as run

    nc = bacc.Bacc("TRN2", target_bir_lowering=False, num_devices=1)
    arrays, args = {}, []
    given = {name: np.ascontiguousarray(inputs[name]) for name in _INS}
    given["shape_constants"] = shape_constants()
    given["layer_constants"] = layer_constants()
    for name, a in given.items():
        arrays[f"in_{name}"] = a
        args.append(nc.dram_tensor(f"in_{name}", a.shape, mybir.dt.from_np(a.dtype), kind="ExternalInput").ap())
    for i, shape in enumerate(_OUTS):
        args.append(nc.dram_tensor(f"out_{i}", shape, F32, kind="ExternalOutput").ap())
    build(nc, *args)
    r = run(nc, [arrays], core_ids=[0])
    return tuple(r.results[0][f"out_{i}"] for i in range(len(_OUTS)))
```
